# Optimizing a Trainium2 kernel written in Bass

```python
import jax, jax.numpy as jnp
from jax import lax
import numpy as np

D_MODEL = 2048
BATCH = 1
SEQ = 256
DEPTH = 1

N_MIXERS = 4
Q_BLOCK = 128
EPS = 1e-6
FOX_HEADS = 16
FOX_HEAD_DIM = D_MODEL // FOX_HEADS
LRU_WIDTH = 2688
LRU_BLOCKS = 16
LRU_BLOCK_DIM = LRU_WIDTH // LRU_BLOCKS
CONV_WIDTH = 4
LRU_C = 8.0
SB_HEADS = 16
SB_HEAD_DIM = D_MODEL // SB_HEADS
MLSTM_HEADS = 4
MLSTM_QK_DIM = D_MODEL // 2 // MLSTM_HEADS
MLSTM_V_DIM = D_MODEL // MLSTM_HEADS
MLSTM_CHUNK = 64
MLSTM_M_INIT = -1e30
D_FF = 4 * D_MODEL


def _n_of(m):
    return (DEPTH - m + N_MIXERS - 1) // N_MIXERS

def rmsnorm(x, g):
    xf = x.astype(jnp.float32)
    y = xf * lax.rsqrt(jnp.mean(xf * xf, axis=-1, keepdims=True) + EPS)
    return (y * g.astype(jnp.float32)).astype(x.dtype)

def _heads(t, n_heads, d):
    b, s, _ = t.shape
    return t.reshape(b, s, n_heads, d).transpose(0, 2, 1, 3)

def _blocks_to_seq(out):
    nb, b, h, q, d = out.shape
    return out.transpose(1, 0, 3, 2, 4).reshape(b, nb * q, h * d)

def fox_attention(x, w_in, b_f, w_out):
    B, S, _ = x.shape
    H, dh = FOX_HEADS, FOX_HEAD_DIM
    proj = x @ w_in
    q, k, v, f_pre = jnp.split(proj, [D_MODEL, 2 * D_MODEL, 3 * D_MODEL], axis=-1)
    q, k, v = _heads(q, H, dh), _heads(k, H, dh), _heads(v, H, dh)
    log_f = jax.nn.log_sigmoid((f_pre + b_f).astype(jnp.float32)).transpose(0, 2, 1)
    cum = jnp.cumsum(log_f, axis=-1)
    nb = S // Q_BLOCK
    qb = q.reshape(B, H, nb, Q_BLOCK, dh).transpose(2, 0, 1, 3, 4)
    cb = cum.reshape(B, H, nb, Q_BLOCK).transpose(2, 0, 1, 3)
    pos_k = jnp.arange(S)
    scale = dh ** -0.5

    def block(args):
        i, q_i, c_i = args
        pos_q = i * Q_BLOCK + jnp.arange(Q_BLOCK)
        logits = jnp.einsum('bhqd,bhkd->bhqk', q_i, k).astype(jnp.float32) * scale
        logits = logits + c_i[..., :, None] - cum[..., None, :]
        logits = jnp.where(pos_k[None, :] <= pos_q[:, None], logits, -jnp.inf)
        p = jax.nn.softmax(logits, axis=-1)
        return jnp.einsum('bhqk,bhkd->bhqd', p.astype(v.dtype), v)

    out = lax.map(block, (jnp.arange(nb), qb, cb))
    return (_blocks_to_seq(out) @ w_out).astype(x.dtype)

def rglru_block(x, w_in, conv_w, conv_b, w_r, b_r, w_i, b_i, lam, w_out):
    B, S, _ = x.shape
    W, NB, bd = LRU_WIDTH, LRU_BLOCKS, LRU_BLOCK_DIM
    proj = x @ w_in
    gate, u = jnp.split(proj, [W], axis=-1)
    u_pad = jnp.pad(u, ((0, 0), (CONV_WIDTH - 1, 0), (0, 0)))
    u = conv_b + sum(u_pad[:, j:j + S, :] * conv_w[j] for j in range(CONV_WIDTH))
    ub = u.reshape(B, S, NB, bd)
    r = jax.nn.sigmoid((jnp.einsum('bsnd,nde->bsne', ub, w_r).reshape(B, S, W) + b_r).astype(jnp.float32))
    ig = jax.nn.sigmoid((jnp.einsum('bsnd,nde->bsne', ub, w_i).reshape(B, S, W) + b_i).astype(jnp.float32))
    log_a = LRU_C * r * jax.nn.log_sigmoid(lam.astype(jnp.float32))
    a = jnp.exp(log_a)
    bterm = jnp.sqrt(-jnp.expm1(2.0 * log_a)) * (ig * u.astype(jnp.float32))

    def combine(left, right):
        a1, b1 = left
        a2, b2 = right
        return a1 * a2, a2 * b1 + b2

    _, h = lax.associative_scan(combine, (a, bterm), axis=1)
    y = h * jax.nn.gelu(gate.astype(jnp.float32))
    return (y.astype(x.dtype) @ w_out).astype(x.dtype)

def stick_breaking_attention(x, w_in, w_out):
    B, S, _ = x.shape
    H, dh = SB_HEADS, SB_HEAD_DIM
    q, k, v = jnp.split(x @ w_in, 3, axis=-1)
    q, k, v = _heads(q, H, dh), _heads(k, H, dh), _heads(v, H, dh)
    nb = S // Q_BLOCK
    qb = q.reshape(B, H, nb, Q_BLOCK, dh).transpose(2, 0, 1, 3, 4)
    pos_k = jnp.arange(S)
    scale = dh ** -0.5

    def block(args):
        i, q_i = args
        pos_q = i * Q_BLOCK + jnp.arange(Q_BLOCK)
        strict = pos_k[None, :] < pos_q[:, None]
        z = jnp.einsum('bhqd,bhkd->bhqk', q_i, k).astype(jnp.float32) * scale
        log_beta = jax.nn.log_sigmoid(z)
        log_1mb = jnp.where(strict, jax.nn.log_sigmoid(-z), 0.0)
        after = lax.cumsum(log_1mb, axis=3, reverse=True) - log_1mb
        att = jnp.where(strict, jnp.exp(log_beta + after), 0.0)
        return jnp.einsum('bhqk,bhkd->bhqd', att.astype(v.dtype), v)

    out = lax.map(block, (jnp.arange(nb), qb))
    return (_blocks_to_seq(out) @ w_out).astype(x.dtype)

def mlstm_block(x, w_in, b_if, head_g, w_out):
    B, S, _ = x.shape
    H, dk, dv, L = MLSTM_HEADS, MLSTM_QK_DIM, MLSTM_V_DIM, MLSTM_CHUNK
    qk = H * dk
    proj = x @ w_in
    q, k, v, o_pre, g_pre = jnp.split(proj, [qk, 2 * qk, 2 * qk + D_MODEL, 2 * qk + 2 * D_MODEL], axis=-1)
    q, k, v = _heads(q, H, dk), _heads(k, H, dk) * (dk ** -0.5), _heads(v, H, dv)
    g_pre = g_pre.astype(jnp.float32).reshape(B, S, 2, H) + b_if.astype(jnp.float32)
    i_pre = g_pre[:, :, 0].transpose(0, 2, 1)
    log_f = jax.nn.log_sigmoid(g_pre[:, :, 1]).transpose(0, 2, 1)
    nc = S // L

    def chunks(t):
        return jnp.moveaxis(t.reshape(t.shape[:2] + (nc, L) + t.shape[3:]), 2, 0)

    causal = jnp.tril(jnp.ones((L, L), dtype=bool))

    def step(carry, xs):
        C, n, m = carry
        qc, kc, vc, lfc, ic = xs
        b = jnp.cumsum(lfc, axis=-1)
        g = b[..., -1]
        Dm = jnp.where(causal, b[..., :, None] - b[..., None, :] + ic[..., None, :], -jnp.inf)
        inter = b + m[..., None]
        m_t = jnp.maximum(inter, jnp.max(Dm, axis=-1))
        w_intra = jnp.exp(Dm - m_t[..., None])
        w_inter = jnp.exp(inter - m_t)
        s = jnp.einsum('bhtd,bhsd->bhts', qc, kc).astype(jnp.float32) * w_intra
        num = (w_inter[..., None] * jnp.einsum('bhtd,bhde->bhte', qc, C)
               + jnp.einsum('bhts,bhse->bhte', s, vc))
        den = w_inter * jnp.einsum('bhtd,bhd->bht', qc, n) + jnp.sum(s, axis=-1)
        h = num / jnp.maximum(jnp.abs(den), jnp.exp(-m_t))[..., None]
        wk = g[..., None] - b + ic
        m_new = jnp.maximum(g + m, jnp.max(wk, axis=-1))
        decay = jnp.exp(g + m - m_new)
        wk_e = jnp.exp(wk - m_new[..., None])
        C_new = decay[..., None, None] * C + jnp.einsum('bhs,bhsd,bhse->bhde', wk_e, kc, vc)
        n_new = decay[..., None] * n + jnp.einsum('bhs,bhsd->bhd', wk_e, kc)
        return (C_new, n_new, m_new), h

    init = (jnp.zeros((B, H, dk, dv), jnp.float32), jnp.zeros((B, H, dk), jnp.float32),
            jnp.full((B, H), MLSTM_M_INIT, jnp.float32))
    _, hs = lax.scan(step, init, (chunks(q), chunks(k), chunks(v), chunks(log_f), chunks(i_pre)))
    h = hs.transpose(1, 0, 3, 2, 4).reshape(B, S, H, dv)
    hn = rmsnorm(h, head_g.reshape(H, dv)).reshape(B, S, D_MODEL)
    y = jax.nn.sigmoid(o_pre.astype(jnp.float32)) * hn
    return (y.astype(x.dtype) @ w_out).astype(x.dtype)

def sqrelu_mlp(x, w1, w2):
    return (jnp.square(jax.nn.relu(x @ w1)) @ w2).astype(x.dtype)

def _dense(key, shape, fan_in):
    return jax.random.normal(key, shape, jnp.float32) * (fan_in ** -0.5)

def first_inputs(seed: int = 0) -> dict:
    key = jax.random.key(seed)
    ks = jax.random.split(key, 24)
    n0, n1, n2, n3 = _n_of(0), _n_of(1), _n_of(2), _n_of(3)
    D, W, NB, bd = D_MODEL, LRU_WIDTH, LRU_BLOCKS, LRU_BLOCK_DIM
    x = jax.random.normal(ks[0], (BATCH, SEQ, D), jnp.float32)
    norm_g = 1.0 + 0.02 * jax.random.normal(ks[1], (DEPTH, 4, D), jnp.float32)
    mlp_w1 = _dense(ks[2], (DEPTH, D, D_FF), D)
    mlp_w2 = _dense(ks[3], (DEPTH, D_FF, D), D_FF)
    fox_w_in = _dense(ks[4], (n0, D, 3 * D + FOX_HEADS), D)
    fox_b_f = 3.0 + 0.1 * jax.random.normal(ks[5], (n0, FOX_HEADS), jnp.float32)
    fox_w_out = _dense(ks[6], (n0, D, D), D)
    lru_w_in = _dense(ks[7], (n1, D, 2 * W), D)
    lru_conv_w = _dense(ks[8], (n1, CONV_WIDTH, W), CONV_WIDTH)
    lru_conv_b = 0.01 * jax.random.normal(ks[9], (n1, W), jnp.float32)
    lru_w_r = _dense(ks[10], (n1, NB, bd, bd), bd)
    lru_b_r = 0.01 * jax.random.normal(ks[11], (n1, W), jnp.float32)
    lru_w_i = _dense(ks[12], (n1, NB, bd, bd), bd)
    lru_b_i = 0.01 * jax.random.normal(ks[13], (n1, W), jnp.float32)
    a_c = jax.random.uniform(ks[14], (n1, W), jnp.float32, minval=0.9, maxval=0.999)
    p = a_c ** (1.0 / LRU_C)
    lru_lambda = jnp.log(p) - jnp.log1p(-p)
    lru_w_out = _dense(ks[15], (n1, W, D), W)
    sb_w_in = _dense(ks[16], (n2, D, 3 * D), D)
    sb_w_out = _dense(ks[17], (n2, D, D), D)
    mlstm_w_in = _dense(ks[18], (n3, D, 3 * D + 2 * MLSTM_HEADS), D)
    mlstm_b_if = jnp.stack([-1.0 + 0.1 * jax.random.normal(ks[19], (n3, MLSTM_HEADS), jnp.float32),
                            3.0 + 0.1 * jax.random.normal(ks[20], (n3, MLSTM_HEADS), jnp.float32)], axis=1)
    mlstm_head_g = 1.0 + 0.02 * jax.random.normal(ks[21], (n3, D), jnp.float32)
    mlstm_w_out = _dense(ks[22], (n3, D, D), D)
    return {'x': x, 'norm_g': norm_g, 'mlp_w1': mlp_w1, 'mlp_w2': mlp_w2,
            'fox_w_in': fox_w_in, 'fox_b_f': fox_b_f, 'fox_w_out': fox_w_out,
            'lru_w_in': lru_w_in, 'lru_conv_w': lru_conv_w, 'lru_conv_b': lru_conv_b,
            'lru_w_r': lru_w_r, 'lru_b_r': lru_b_r, 'lru_w_i': lru_w_i, 'lru_b_i': lru_b_i,
            'lru_lambda': lru_lambda, 'lru_w_out': lru_w_out,
            'sb_w_in': sb_w_in, 'sb_w_out': sb_w_out,
            'mlstm_w_in': mlstm_w_in, 'mlstm_b_if': mlstm_b_if, 'mlstm_head_g': mlstm_head_g,
            'mlstm_w_out': mlstm_w_out}

def first_block(x, norm_g, mlp_w1, mlp_w2, fox_w_in, fox_b_f, fox_w_out,
              lru_w_in, lru_conv_w, lru_conv_b, lru_w_r, lru_b_r, lru_w_i, lru_b_i,
              lru_lambda, lru_w_out, sb_w_in, sb_w_out,
              mlstm_w_in, mlstm_b_if, mlstm_head_g, mlstm_w_out):
    for i in range(DEPTH):
        m, j = i % N_MIXERS, i // N_MIXERS
        h = rmsnorm(x, norm_g[i, 0])
        if m == 0:
            h = fox_attention(h, fox_w_in[j], fox_b_f[j], fox_w_out[j])
        elif m == 1:
            h = rglru_block(h, lru_w_in[j], lru_conv_w[j], lru_conv_b[j], lru_w_r[j], lru_b_r[j],
                            lru_w_i[j], lru_b_i[j], lru_lambda[j], lru_w_out[j])
        elif m == 2:
            h = stick_breaking_attention(h, sb_w_in[j], sb_w_out[j])
        else:
            h = mlstm_block(h, mlstm_w_in[j], mlstm_b_if[j], mlstm_head_g[j], mlstm_w_out[j])
        x = x + rmsnorm(h, norm_g[i, 1])
        h = sqrelu_mlp(rmsnorm(x, norm_g[i, 2]), mlp_w1[i], mlp_w2[i])
        x = x + rmsnorm(h, norm_g[i, 3])
    return x


N_ATT_HEADS = 8
HEAD_DIM = 128
ATT_WIDTH = N_ATT_HEADS * HEAD_DIM
MOBA_BLOCK = 256
MOBA_TOPK = 3
Q_CHUNK = 128
N_SGU_GROUPS = 8
SGU_GROUP_DIM = 128
SGU_WIDTH = N_SGU_GROUPS * SGU_GROUP_DIM
SGU_CHUNK = 128
IN_SPLITS = (ATT_WIDTH, ATT_WIDTH, ATT_WIDTH, ATT_WIDTH,
             SGU_WIDTH, SGU_WIDTH, SGU_WIDTH,
             D_MODEL, D_MODEL)
IN_WIDTH = 4 * ATT_WIDTH + 3 * SGU_WIDTH + 2 * D_MODEL
NEG_INF = -1e30


def rms_norm(x, g):
    xf = x.astype(jnp.float32)
    y = xf * lax.rsqrt(jnp.mean(xf * xf, axis=-1, keepdims=True) + EPS)
    return (y * g.astype(jnp.float32)).astype(x.dtype)

def moba_attention(q, k, v):
    B, S, H, Dh = q.shape
    nb = -(-S // MOBA_BLOCK)
    s_pad = nb * MOBA_BLOCK
    topk = min(MOBA_TOPK, nb)
    nc = S // Q_CHUNK
    scale = Dh ** -0.5

    qh = q.transpose(0, 2, 1, 3)
    pad = ((0, 0), (0, 0), (0, s_pad - S), (0, 0))
    kh = jnp.pad(k.transpose(0, 2, 1, 3), pad)
    vh = jnp.pad(v.transpose(0, 2, 1, 3), pad)
    k_blocks = kh.reshape(B, H, nb, MOBA_BLOCK, Dh)
    v_blocks = vh.reshape(B, H, nb, MOBA_BLOCK, Dh)
    k_mean = jnp.mean(k_blocks.astype(jnp.float32), axis=3)
    q_chunks = qh.reshape(B, H, nc, Q_CHUNK, Dh).transpose(2, 0, 1, 3, 4)

    bi = jnp.arange(B)[:, None, None, None]
    hi = jnp.arange(H)[None, :, None, None]
    blk_ids = jnp.arange(nb)

    def one_chunk(args):
        qc, c = args
        q_pos = c * Q_CHUNK + jnp.arange(Q_CHUNK)
        cur = (c * Q_CHUNK) // MOBA_BLOCK
        gate = jnp.einsum('bhqd,bhnd->bhqn', qc.astype(jnp.float32), k_mean)
        gate = jnp.where(blk_ids < cur, gate, NEG_INF)
        _, idx = lax.top_k(gate, topk)
        valid = idx < cur
        k_sel = k_blocks[bi, hi, idx]
        v_sel = v_blocks[bi, hi, idx]
        s_past = jnp.einsum('bhqd,bhqknd->bhqkn', qc, k_sel,
                            preferred_element_type=jnp.float32) * scale
        s_past = jnp.where(valid[..., None], s_past, NEG_INF)
        k_own = lax.dynamic_index_in_dim(k_blocks, cur, axis=2, keepdims=False)
        v_own = lax.dynamic_index_in_dim(v_blocks, cur, axis=2, keepdims=False)
        s_own = jnp.einsum('bhqd,bhnd->bhqn', qc, k_own,
                           preferred_element_type=jnp.float32) * scale
        key_pos = cur * MOBA_BLOCK + jnp.arange(MOBA_BLOCK)
        s_own = jnp.where(key_pos[None, :] <= q_pos[:, None], s_own, NEG_INF)
        logits = jnp.concatenate(
            [s_past.reshape(B, H, Q_CHUNK, topk * MOBA_BLOCK), s_own], axis=-1)
        p = jax.nn.softmax(logits, axis=-1)
        p_past = p[..., :topk * MOBA_BLOCK].reshape(B, H, Q_CHUNK, topk, MOBA_BLOCK)
        p_own = p[..., topk * MOBA_BLOCK:]
        o = (jnp.einsum('bhqkn,bhqknd->bhqd', p_past.astype(v_sel.dtype), v_sel)
             + jnp.einsum('bhqn,bhnd->bhqd', p_own.astype(v_own.dtype), v_own))
        return o.astype(qc.dtype)

    out = lax.map(one_chunk, (q_chunks, jnp.arange(nc, dtype=jnp.int32)))
    return out.transpose(1, 0, 3, 2, 4).reshape(B, S, H * Dh)

def spatial_gating(u, v, v_norm_g, w_s, b_s):
    B, S, _ = u.shape
    n = S // SGU_CHUNK
    vg = rms_norm(v.reshape(B, S, N_SGU_GROUPS, SGU_GROUP_DIM), v_norm_g)
    vg = vg.reshape(B, n, SGU_CHUNK, N_SGU_GROUPS, SGU_GROUP_DIM)
    causal = jnp.tril(jnp.ones((SGU_CHUNK, SGU_CHUNK), dtype=bool))
    w = jnp.where(causal[None], w_s, jnp.zeros((), w_s.dtype))
    mixed = jnp.einsum('gts,bnsgc->bntgc', w, vg) + b_s.T[:, :, None]
    return u * mixed.reshape(B, S, SGU_WIDTH)

def hybrid_layer(x, norm_g, w_in, q_norm_g, k_norm_g, sgu_norm_g, w_s, b_s,
                 w_proj_a, w_proj_b, w_out):
    B, S, _ = x.shape
    h = rms_norm(x, norm_g)
    proj = h @ w_in
    cuts = [int(c) for c in np.cumsum(IN_SPLITS)[:-1]]
    q, k, v, z_a, u_b, v_b, z_b, g_a, g_b = jnp.split(proj, cuts, axis=-1)
    q = rms_norm(q.reshape(B, S, N_ATT_HEADS, HEAD_DIM), q_norm_g)
    k = rms_norm(k.reshape(B, S, N_ATT_HEADS, HEAD_DIM), k_norm_g)
    v = v.reshape(B, S, N_ATT_HEADS, HEAD_DIM)
    att = moba_attention(q, k, v)
    y_a = (att * jax.nn.silu(z_a)) @ w_proj_a
    sgu = spatial_gating(jax.nn.gelu(u_b), jax.nn.gelu(v_b), sgu_norm_g, w_s, b_s)
    y_b = (sgu * jax.nn.silu(z_b)) @ w_proj_b
    merged = jax.nn.sigmoid(g_a) * y_a + jax.nn.sigmoid(g_b) * y_b
    return x + merged @ w_out

def second_inputs(seed: int = 0) -> dict:
    key = jax.random.key(seed)
    ks = jax.random.split(key, 12)
    f32 = jnp.float32
    x = jax.random.normal(ks[0], (BATCH, SEQ, D_MODEL), f32)
    norm_g = 1.0 + 0.02 * jax.random.normal(ks[1], (DEPTH, D_MODEL), f32)
    w_in = jax.random.normal(ks[2], (DEPTH, D_MODEL, IN_WIDTH), f32) * D_MODEL ** -0.5
    q_norm_g = 1.0 + 0.02 * jax.random.normal(ks[3], (DEPTH, HEAD_DIM), f32)
    k_norm_g = 1.0 + 0.02 * jax.random.normal(ks[4], (DEPTH, HEAD_DIM), f32)
    sgu_norm_g = 1.0 + 0.02 * jax.random.normal(ks[5], (DEPTH, SGU_GROUP_DIM), f32)
    w_spatial = jax.random.normal(ks[6], (DEPTH, N_SGU_GROUPS, SGU_CHUNK, SGU_CHUNK), f32) * SGU_CHUNK ** -0.5
    b_spatial = 1.0 + 0.1 * jax.random.normal(ks[7], (DEPTH, N_SGU_GROUPS, SGU_CHUNK), f32)
    w_proj_a = jax.random.normal(ks[8], (DEPTH, ATT_WIDTH, D_MODEL), f32) * ATT_WIDTH ** -0.5
    w_proj_b = jax.random.normal(ks[9], (DEPTH, SGU_WIDTH, D_MODEL), f32) * SGU_WIDTH ** -0.5
    w_out = jax.random.normal(ks[10], (DEPTH, D_MODEL, D_MODEL), f32) * D_MODEL ** -0.5
    return {"x": x, "norm_g": norm_g, "w_in": w_in, "q_norm_g": q_norm_g,
            "k_norm_g": k_norm_g, "sgu_norm_g": sgu_norm_g, "w_spatial": w_spatial,
            "b_spatial": b_spatial, "w_proj_a": w_proj_a, "w_proj_b": w_proj_b,
            "w_out": w_out}

def second_block(x, norm_g, w_in, q_norm_g, k_norm_g, sgu_norm_g, w_spatial, b_spatial,
              w_proj_a, w_proj_b, w_out):
    for l in range(DEPTH):
        x = hybrid_layer(x, norm_g[l], w_in[l], q_norm_g[l], k_norm_g[l], sgu_norm_g[l],
                         w_spatial[l], b_spatial[l], w_proj_a[l], w_proj_b[l], w_out[l])
    return x


def setup_inputs(seed=0):
    out = dict(first_inputs(seed))
    for name, value in second_inputs(seed + 1).items():
        if name != "x":
            out[name + "_2"] = value
    return out


def reference(
    x, norm_g, mlp_w1, mlp_w2, fox_w_in, fox_b_f, fox_w_out, lru_w_in, lru_conv_w, lru_conv_b,
    lru_w_r, lru_b_r, lru_w_i, lru_b_i, lru_lambda, lru_w_out, sb_w_in, sb_w_out, mlstm_w_in,
    mlstm_b_if, mlstm_head_g, mlstm_w_out, norm_g_2, w_in_2, q_norm_g_2, k_norm_g_2,
    sgu_norm_g_2, w_spatial_2, b_spatial_2, w_proj_a_2, w_proj_b_2, w_out_2,
):
    x = first_block(
        x, norm_g, mlp_w1, mlp_w2, fox_w_in, fox_b_f, fox_w_out, lru_w_in, lru_conv_w,
        lru_conv_b, lru_w_r, lru_b_r, lru_w_i, lru_b_i, lru_lambda, lru_w_out, sb_w_in,
        sb_w_out, mlstm_w_in, mlstm_b_if, mlstm_head_g, mlstm_w_out,
    )
    return second_block(
        x, norm_g_2, w_in_2, q_norm_g_2, k_norm_g_2, sgu_norm_g_2, w_spatial_2, b_spatial_2,
        w_proj_a_2, w_proj_b_2, w_out_2,
    )


_drawn_inputs = setup_inputs


def setup_inputs(seed=0):
    import zlib

    import numpy as np

    out = dict(_drawn_inputs(seed))
    spreads = {}
    factors = {'norm_g_2': 8.0,
     'q_norm_g_2': 25.024,
     'k_norm_g_2': 26.042,
     'sgu_norm_g_2': 27.012,
     'b_spatial_2': 4.703}
    for name, (base, spread) in spreads.items():
        noise = np.random.default_rng([zlib.crc32(name.encode()), seed]).standard_normal(out[name].shape)
        drawn = base * np.exp(spread * noise) if base else spread * noise
        out[name] = __import__('jax').numpy.asarray(drawn.astype(out[name].dtype))
    for name, factor in factors.items():
        out[name] = (out[name] * factor).astype(out[name].dtype)
    return out
```

```python
from contextlib import ExitStack

import concourse.bass as bass
from concourse import mybir

ALU = mybir.AluOpType
ACT = mybir.ActivationFunctionType
AX = mybir.AxisListType
F32 = mybir.dt.float32
F32R = mybir.dt.float32r

P = 128
TOK = 256
NT = TOK // P
D = 2048
KT = D // P
FOX_HEADS = 16
MOBA_HEADS = 8
FF_GROUPS = 4
CHUNK = 1024
RING = 4
TILE_CHUNKS = 2
GROUP_CHUNKS = 8
GROUP_COLS = 512
EPS = 1e-6
SCALE = float(P) ** -0.5
NEG = -1e30
GELU_CUBE = 0.044715
GELU_SCALE = 0.7978845608028654

PHASES = [("fox_v", 32), ("fox_qk", 64), ("fox_out", 32), ("mlp", 256), ("qkv", 64), ("sgu_uz", 48),
          ("gates", 64), ("proj_b", 16), ("proj_a", 16), ("out", 32)]
FIRST = {}
for _name, _n in PHASES:
    FIRST[_name] = sum(n for m, n in PHASES[:len(FIRST)])
N_CHUNKS = sum(n for _, n in PHASES)
TILES_BEFORE = {"fox_qk": 0, "mlp": 32, "sgu_uz": 96, "gates": 120, "proj_b": 152, "proj_a": 168}
GROUPS_BEFORE = {"fox_v": 0, "fox_out": 4, "mlp": 8, "qkv": 24, "out": 32}


def one(ap, index):
    if isinstance(index, int):
        return ap[:, index, :]
    return ap[:, bass.ds(index, 1), :].rearrange("p a n -> p (a n)")


def build(nc, stream, x, fox_w_f, fox_b_f, norm_rows, norm_cols, w_spatial, b_spatial, head_cols, out):
    fox_scratch = nc.dram_tensor("cum_rows", (FOX_HEADS, TOK), F32, kind="Internal").ap()

    with ExitStack() as ctx:
        def sb(name, shape, dt=F32):
            return ctx.enter_context(nc.sbuf_tensor(name, shape, dt))

        def sem(name):
            return ctx.enter_context(nc.semaphore(name))

        raw = sb("raw", [P, RING, CHUNK])
        w_hi = sb("w_hi", [P, RING, CHUNK], F32R)
        w_lo = sb("w_lo", [P, RING, CHUNK], F32R)
        res = sb("res", [P, NT, D])
        h_hi = sb("h_hi", [P, KT, TOK], F32R)
        h_lo = sb("h_lo", [P, KT, TOK], F32R)
        a_hi = sb("a_hi", [P, KT, TOK], F32R)
        a_lo = sb("a_lo", [P, KT, TOK], F32R)
        wide = sb("wide", [P, 6144])
        gate = sb("gate", [P, 32, TOK])
        rowg = sb("rowg", [P, D])
        ident = sb("ident", [P, P])
        mask = sb("mask", [P, 384])
        bias = sb("bias", [P, 384])
        logit = sb("logit", [P, 384])
        prob = sb("prob", [P, 384])
        probT = sb("probT", [P, 384])
        q_head = sb("q_head", [P, TOK])
        k_head = sb("k_head", [P, TOK])
        v_head = sb("v_head", [P, NT, P])
        qk_norm = sb("qk_norm", [P, 4, P])
        att_f = sb("att_f", [P, TOK])
        neg_max = sb("neg_max", [P, 2])
        row_sum = sb("row_sum", [P, 2])
        row_inv = sb("row_inv", [P, 2])
        cols = sb("cols", [P, 3, KT])
        hcols = sb("hcols", [P, 3])
        hscale = sb("hscale", [P, 3])
        sq_sum = sb("sq_sum", [P, NT, 4])
        sq_all = sb("sq_all", [P, 2])
        mean_sq = sb("mean_sq", [P, 2])
        rstd = sb("rstd", [P, 2])
        half_neg = sb("half_neg", [P, 48])
        cum_cols = sb("cum_cols", [P, NT, FOX_HEADS])
        head_sq = sb("head_sq", [P, NT, 24])
        head_rstd = sb("head_rstd", [P, NT, 24])
        vb_sq = sb("vb_sq", [P, NT, 8])
        vb_rstd = sb("vb_rstd", [P, NT, 8])

        group_sum = wide[:, 0:NT * D].rearrange("p (t n) -> p t n", t=NT)
        qkv = wide[:, :].rearrange("p (t n) -> p t n", t=NT)
        merge_b = wide[:, 0:KT * TOK].rearrange("p (k t) -> p k t", k=KT)
        spare = wide[:, 4096:6144]
        xs = [spare[:, b * 512:(b + 1) * 512].rearrange("p (t n) -> p t n", t=NT) for b in range(2)]
        junk = spare[:, 1024:1536]
        merge_t = [spare[:, b * 256:(b + 1) * 256] for b in range(2)]
        merge_s = [spare[:, 512 + b * 256:768 + b * 256] for b in range(2)]
        w_f = spare[:, 1024:1280].rearrange("p (k h) -> p k h", k=KT)
        b_f = spare[:, 1280:1312].rearrange("p (t h) -> p t h", t=NT)
        f_z, f_abs, f_min, f_exp, f_ln, f_log = [
            spare[:, 1312 + 32 * n:1344 + 32 * n].rearrange("p (t h) -> p t h", t=NT) for n in range(6)]
        cum_neg = spare[0:FOX_HEADS, 1504:1760]
        tri = spare[:, 0:512].rearrange("p (b t) -> p b t", b=NT)
        gate_flat = gate[:, :, :].rearrange("p k t -> p (k t)")
        fox_v = gate_flat[:, 0:4096].rearrange("p (t n) -> p t n", t=NT)
        cum_rows = gate_flat[:, 4096:8192].rearrange("p (h t) -> p h t", h=FOX_HEADS)
        relu = [gate_flat[:, b * 256:(b + 1) * 256] for b in range(2)]
        relu2 = [gate_flat[:, 512 + b * 256:768 + b * 256] for b in range(2)]
        vb = gate_flat[:, 0:2048].rearrange("p (t n) -> p t n", t=NT)
        u_gelu = gate_flat[:, 2048:4096].rearrange("p (g t) -> p g t", g=8)
        w_s = gate_flat[:, 4096:5120].rearrange("p (g t) -> p g t", g=8)
        b_s = gate_flat[:, 5120:6144].rearrange("p (g t) -> p g t", g=8)
        gelu_a = gate_flat[:, 6144:7168].rearrange("p (t n) -> p t n", t=NT)
        gelu_b = gate_flat[:, 7168:8192].rearrange("p (t n) -> p t n", t=NT)
        uz_a = [gate_flat[:, 6144 + b * 256:6400 + b * 256] for b in range(2)]
        uz_b = [gate_flat[:, 6656 + b * 256:6912 + b * 256] for b in range(2)]
        mixed = gate_flat[:, 7168:7424]
        vb_head = gate_flat[:, 7424:7680].rearrange("p (t n) -> p t n", t=NT)
        za_silu = rowg[:, :].rearrange("p (g t) -> p g t", g=8)

        bank = [ctx.enter_context(nc.psum_tensor(f"bank{n}", [P, 512], F32)) for n in range(8)]
        tile_sum = bank[0:2]
        group_bank = [bank[2:4], bank[4:6]]
        pv_sum = bank[4]
        score = bank[6]
        turned = bank[7]

        raw_landed = [sem(f"raw_landed{n}") for n in range(RING)]
        hi_ready = sem("hi_ready")
        lo_ready = sem("lo_ready")
        chunk_done = sem("chunk_done")
        tile_taken = [sem("tile_taken0"), sem("tile_taken1")]
        group_taken = [sem("group_taken0"), sem("group_taken1")]
        consts_in = sem("consts_in")
        x_in = sem("x_in")
        fox_in = sem("fox_in")
        rowg_in = sem("rowg_in")
        sgu_in = sem("sgu_in")
        w_s_ready = sem("w_s_ready")
        consts_made = sem("consts_made")
        tri_made = sem("tri_made")
        scale_made = sem("scale_made")
        sumsq_ready = sem("sumsq_ready")
        mean_ready = sem("mean_ready")
        var_ready = sem("var_ready")
        rstd_ready = sem("rstd_ready")
        xs_ready = sem("xs_ready")
        xt_done = sem("xt_done")
        xt_hi = sem("xt_hi")
        h_ready = sem("h_ready")
        group_sq = sem("group_sq")
        group_in = sem("group_in")
        group_gained = sem("group_gained")
        res_added = sem("res_added")
        wf_hi = sem("wf_hi")
        wf_ready = sem("wf_ready")
        f_done = sem("f_done")
        f_step = sem("f_step")
        f_exp_ready = sem("f_exp_ready")
        f_log_ready = sem("f_log_ready")
        cum_done = sem("cum_done")
        cum_ready = sem("cum_ready")
        cum_out = sem("cum_out")
        cum_in = sem("cum_in")
        v_ready = sem("v_ready")
        q_ready = sem("q_ready")
        k_ready = sem("k_ready")
        bias_step = sem("bias_step")
        bias_ready = sem("bias_ready")
        v_head_ready = sem("v_head_ready")
        s_done = sem("s_done")
        logit_ready = sem("logit_ready")
        max_ready = sem("max_ready")
        exp_ready = sem("exp_ready")
        inv_ready = sem("inv_ready")
        prob_ready = sem("prob_ready")
        t_done = sem("t_done")
        probT_ready = sem("probT_ready")
        pv_done = sem("pv_done")
        att_f_ready = sem("att_f_ready")
        att_hi = sem("att_hi")
        att_ready = sem("att_ready")
        relu_ready = sem("relu_ready")
        relu2_ready = sem("relu2_ready")
        ff_hi = sem("ff_hi")
        ff_ready = sem("ff_ready")
        ff_sum_ready = sem("ff_sum_ready")
        ff_sq = sem("ff_sq")
        zeroed = sem("zeroed")
        vb_sq1 = sem("vb_sq1")
        vb_step = sem("vb_step")
        vb_cube = sem("vb_cube")
        vb_tanh = sem("vb_tanh")
        vb_gelu = sem("vb_gelu")
        vb_sq2 = sem("vb_sq2")
        vb_sums = sem("vb_sums")
        qkv_sq = sem("qkv_sq")
        qkv_in = sem("qkv_in")
        qkv_sums = sem("qkv_sums")
        hvar = sem("hvar")
        hr_ready = sem("hr_ready")
        vb_head_ready = sem("vb_head_ready")
        mix_done = sem("mix_done")
        uz_sq = sem("uz_sq")
        uz_step = sem("uz_step")
        uz_cube = sem("uz_cube")
        uz_tanh = sem("uz_tanh")
        u_ready = sem("u_ready")
        mixed_ready = sem("mixed_ready")
        zb_tanh = sem("zb_tanh")
        zb_silu = sem("zb_silu")
        zb_gated = sem("zb_gated")
        sgu_f = sem("sgu_f")
        sgu_hi = sem("sgu_hi")
        sgu_ready = sem("sgu_ready")
        za_tanh = sem("za_tanh")
        za_ready = sem("za_ready")
        qk_norm_ready = sem("qk_norm_ready")
        qk_turned = sem("qk_turned")
        gate_ready = sem("gate_ready")
        mb_ready = sem("mb_ready")
        ma_ready = sem("ma_ready")
        merged_f = sem("merged_f")
        merged_hi = sem("merged_hi")
        merged_ready = sem("merged_ready")
        out_ready = sem("out_ready")
        stored = sem("stored")

        block = ctx.enter_context(nc.Block())

        @block.sync
        def _(sp):
            def load(c, slot):
                sp.dma_start(raw[:, slot, :],
                             stream[bass.ds(c, 1), :, :].rearrange("a p n -> p (a n)")
                             if not isinstance(c, int) else stream[c, :, :]).then_inc(raw_landed[slot], 16)

            sp.dma_start(res[:, 0, :], x[0, 0:P, :]).then_inc(x_in, 16)
            sp.dma_start(res[:, 1, :], x[0, P:TOK, :]).then_inc(x_in, 16)
            for slot in range(RING):
                load(slot, slot)
            with sp.Fori(1, N_CHUNKS // RING) as j:
                for slot in range(RING):
                    sp.wait_ge(lo_ready, j * RING + (slot + 1 - RING))
                    load(j * RING + slot, slot)
            for n in range(4):
                for t in range(NT):
                    sp.wait_ge(out_ready, n * NT + t + 1)
                    cols_n = slice(n * GROUP_COLS, (n + 1) * GROUP_COLS)
                    sp.dma_start(out[0, t * P:(t + 1) * P, cols_n], group_sum[:, t, cols_n]).then_inc(stored, 16)
            sp.wait_ge(stored, 16 * 4 * NT)

        @block.tensor
        def _(pe):
            def tile_chunk(c, slot, dst, k0, x_hi, x_lo, first, last):
                pe.wait_ge(lo_ready, c + 1)
                for k in range(8):
                    w = slice(k * P, (k + 1) * P)
                    parts = ((w_hi, x_hi), (w_hi, x_lo), (w_lo, x_hi))
                    for n, (wt, xt) in enumerate(parts):
                        mm = pe.matmul(dst[:, 0:TOK], wt[:, slot, w], xt[:, k0 + k, :],
                                       start=first and k == 0 and n == 0, stop=last and k == 7 and n == 2)
                mm.then_inc(chunk_done, 1)

            def feature_tile(c, slot, taken, b, x_hi, x_lo):
                pe.wait_ge(tile_taken[b], taken + 1)
                for half in range(TILE_CHUNKS):
                    tile_chunk(c + half, slot + half, tile_sum[b], 8 * half, x_hi, x_lo, half == 0, half == 1)

            def group_chunk(c, slot, j, dst, x_hi, x_lo):
                pe.wait_ge(lo_ready, c + 1)
                for k in range(2):
                    w = slice(k * GROUP_COLS, (k + 1) * GROUP_COLS)
                    for t in range(NT):
                        tt = slice(t * P, (t + 1) * P)
                        parts = ((x_hi, w_hi), (x_lo, w_hi), (x_hi, w_lo))
                        for n, (xt, wt) in enumerate(parts):
                            mm = pe.matmul(dst[t][:, :], xt[:, 2 * j + k, tt], wt[:, slot, w],
                                           start=j == 0 and k == 0 and n == 0,
                                           stop=j == GROUP_CHUNKS - 1 and k == 1 and n == 2)
                mm.then_inc(chunk_done, 1)

            def group_pair(c, taken, x_hi, x_lo, before={}, after={}):
                for g in range(2):
                    pe.wait_ge(group_taken[g], taken + 1)
                    for j in range(GROUP_CHUNKS):
                        if g == 0 and j in before:
                            before[j]()
                        group_chunk(c + (g * GROUP_CHUNKS + j), j % RING, j, group_bank[g], x_hi, x_lo)
                        if g == 0 and j in after:
                            after[j]()

            def turn_norm(norm, j):
                n = 8 * norm + j
                pe.wait_ge(xs_ready, 2 * n + 2)
                if n >= 2:
                    pe.wait_ge(h_ready, n - 1)
                for k in range(2):
                    for t in range(NT):
                        to = k * TOK + t * P
                        mm = pe.transpose(bank[6 + n % 2][:, to:to + P], xs[n % 2][:, t, k * P:(k + 1) * P],
                                          ident[:, :])
                mm.then_inc(xt_done, 1)

            def norm_before(norm):
                def first():
                    turn_norm(norm, 0)
                    turn_norm(norm, 1)
                    pe.wait_ge(h_ready, 8 * norm + 1)

                def later(j):
                    def run():
                        if j < 7:
                            turn_norm(norm, j + 1)
                        pe.wait_ge(h_ready, 8 * norm + j + 1)
                    return run
                return {0: first, **{j: later(j) for j in range(1, 8)}}

            def scores(n):
                pe.wait_ge(q_ready, n + 1)
                pe.wait_ge(k_ready, n + 1)
                pe.matmul(score[:, 0:P], q_head[:, 0:P], k_head[:, 0:P], start=True, stop=True)
                pe.matmul(score[:, P:384], q_head[:, P:TOK], k_head[:, :], start=True,
                          stop=True).then_inc(s_done, 1)

            def turn_probs(n):
                pe.wait_ge(prob_ready, 2 * n + 2)
                for b in range(3):
                    mm = pe.transpose(turned[:, b * P:(b + 1) * P], prob[:, b * P:(b + 1) * P], ident[:, :])
                mm.then_inc(t_done, 1)

            def weigh_values(n):
                pe.wait_ge(probT_ready, n + 1)
                pe.wait_ge(v_head_ready, n + 1)
                if not isinstance(n, int) or n >= 1:
                    pe.wait_ge(att_ready, n)
                pe.matmul(pv_sum[:, 0:TOK], v_head[:, 0, :], probT[:, 0:TOK], start=True, stop=False)
                pe.matmul(pv_sum[:, P:TOK], v_head[:, 1, :], probT[:, TOK:384], start=False,
                          stop=True).then_inc(pv_done, 1)

            pe.wait_ge(consts_made, 2)
            group_pair(FIRST["fox_v"], 0, h_hi, h_lo, before=norm_before(0))
            pe.wait_ge(wf_ready, 1)
            for t in range(NT):
                tt = slice(t * P, (t + 1) * P)
                for k in range(KT):
                    parts = ((h_hi, a_hi), (h_lo, a_hi), (h_hi, a_lo))
                    for n, (xt, wt) in enumerate(parts):
                        mm = pe.matmul(score[:, t * 16:(t + 1) * 16], xt[:, k, tt], wt[:, 0, k * 16:(k + 1) * 16],
                                       start=k == 0 and n == 0, stop=k == KT - 1 and n == 2)
            mm.then_inc(f_done, 1)
            group_pair(FIRST["fox_v"] + 16, 1, h_hi, h_lo)
            pe.wait_ge(f_log_ready, 1)
            pe.wait_ge(tri_made, 1)
            for b in range(NT):
                pe.matmul(turned[0:FOX_HEADS, 0:TOK], f_log[:, b, :], tri[:, b, :], start=b == 0, stop=b == 1)
            pe.matmul(turned[:, 256:272], tri[:, 0, 0:P], f_log[:, 0, :], start=True, stop=True)
            pe.matmul(turned[:, 272:288], tri[:, 0, P:TOK], f_log[:, 0, :], start=True, stop=False)
            pe.matmul(turned[:, 272:288], tri[:, 1, P:TOK], f_log[:, 1, :], start=False,
                      stop=True).then_inc(cum_done, 1)

            def fox_head(h, heads_before):
                c = FIRST["fox_qk"] + h * 4
                feature_tile(c, 0, h, 0, h_hi, h_lo)
                if heads_before >= 2:
                    turn_probs(h - 2)
                if heads_before >= 1:
                    scores(h - 1)
                feature_tile(c + 2, 2, h, 1, h_hi, h_lo)
                if heads_before >= 2:
                    weigh_values(h - 2)

            for h in range(3):
                fox_head(h, h)
            with pe.Fori(3, FOX_HEADS) as h:
                fox_head(h, 3)

            def heads_in(j):
                return lambda: pe.wait_ge(att_ready, 2 * j + 2)

            def tail(*steps):
                def run():
                    for step, n in steps:
                        step(n)
                return run

            group_pair(FIRST["fox_out"], 2, a_hi, a_lo, before={j: heads_in(j) for j in range(8)},
                       after={1: tail((turn_probs, 14), (scores, 15)), 3: tail((weigh_values, 14)),
                              5: tail((turn_probs, 15)), 6: tail((weigh_values, 15))})
            group_pair(FIRST["fox_out"] + 16, 3, a_hi, a_lo)

            for j in range(8):
                turn_norm(1, j)
            pe.wait_ge(h_ready, 16)

            def mlp_group(g):
                c = FIRST["mlp"] + g * 64
                with pe.Fori(0, 8) as i:
                    for b in range(2):
                        feature_tile(c + (i * 4 + 2 * b), 2 * b, g * 8 + (i + 16), b, h_hi, h_lo)
                with pe.Fori(0, 2) as i:
                    group_pair(c + (i * 16 + 32), g * 2 + (i + 4), a_hi, a_lo,
                               before={0: lambda: pe.wait_ge(ff_ready, g * 16 + 16)})

            with pe.Fori(0, FF_GROUPS) as g:
                mlp_group(g)

            group_pair(FIRST["qkv"], 12, h_hi, h_lo, before=norm_before(2))
            with pe.Fori(1, 4) as i:
                group_pair(FIRST["qkv"] + i * 16, i + 12, h_hi, h_lo)

            with pe.Fori(0, 4) as i:
                for b in range(2):
                    feature_tile(FIRST["sgu_uz"] + (i * 4 + 2 * b), 2 * b, i + 48, b, h_hi, h_lo)
            with pe.Fori(0, 4) as i:
                for b in range(2):
                    pe.wait_ge(w_s_ready, 1)
                    pe.wait_ge(vb_head_ready, i * 2 + (b + 1))
                    for t in range(NT):
                        mm = pe.matmul(score[:, t * P:(t + 1) * P], vb_head[:, t, :], one(w_s, i * 2 + b),
                                       start=True, stop=True)
                    mm.then_inc(mix_done, 1)
                    feature_tile(FIRST["sgu_uz"] + 16 + (i * 4 + 2 * b), 2 * b, i + 52, b, h_hi, h_lo)
            with pe.Fori(0, 4) as i:
                for b in range(2):
                    feature_tile(FIRST["sgu_uz"] + 32 + (i * 4 + 2 * b), 2 * b, i + 56, b, h_hi, h_lo)

            def gate_head(h, first):
                c = FIRST["gates"] + h * 8
                n = h + FOX_HEADS
                feature_tile(c, 0, h * 2 + 60, 0, h_hi, h_lo)
                if not first:
                    weigh_values(n - 1)
                pe.wait_ge(qk_norm_ready, h * 2 + 2)
                for b in range(4):
                    mm = pe.transpose(turned[:, b * P:(b + 1) * P], qk_norm[:, b, :], ident[:, :])
                mm.then_inc(qk_turned, 1)
                feature_tile(c + 2, 2, h * 2 + 60, 1, h_hi, h_lo)
                scores(n)
                feature_tile(c + 4, 0, h * 2 + 61, 0, h_hi, h_lo)
                feature_tile(c + 6, 2, h * 2 + 61, 1, h_hi, h_lo)
                turn_probs(n)

            gate_head(0, True)
            with pe.Fori(1, MOBA_HEADS) as h:
                gate_head(h, False)
            weigh_values(FOX_HEADS + MOBA_HEADS - 1)

            def project(name, k0):
                with pe.Fori(0, 4) as i:
                    for s in range(4):
                        pe.wait_ge(tile_taken[s % 2], i * 2 + (TILES_BEFORE[name] // 2 + s // 2 + 1))
                        tile_chunk(FIRST[name] + (i * 4 + s), s, tile_sum[s % 2], k0, a_hi, a_lo, True, True)

            pe.wait_ge(sgu_ready, 8)
            project("proj_b", 8)
            pe.wait_ge(att_ready, FOX_HEADS + MOBA_HEADS)
            project("proj_a", 0)

            def merged_in(j):
                return lambda: pe.wait_ge(merged_ready, 2 * j + 2)

            group_pair(FIRST["out"], 16, h_hi, h_lo, before={j: merged_in(j) for j in range(8)})
            group_pair(FIRST["out"] + 16, 17, h_hi, h_lo)

        @block.scalar
        def _(act):
            def split(c, slot, lap):
                act.wait_ge(chunk_done, c + 1)
                act.wait_ge(raw_landed[slot], lap * 16 + 16)
                nc.scalar.activation(w_hi[:, slot, :], raw[:, slot, :], ACT.Copy).then_inc(hi_ready, 1)

            def splits(c, lap, slots):
                for s in slots:
                    split(c + s, s, lap)

            def norm_block(norm, j):
                n = 8 * norm + j
                act.wait_ge(xt_done, n + 1)
                for k in range(2):
                    kt = 2 * j + k
                    nc.scalar.activation(h_hi[:, kt, :], bank[6 + n % 2][:, k * TOK:(k + 1) * TOK], ACT.Copy,
                                         scale=cols[:, norm, kt:kt + 1]).then_inc(xt_hi, 1)

            def exps(n):
                act.wait_ge(max_ready, n * 2 + 2)
                nc.scalar.activation(prob[:, 0:P], logit[:, 0:P], ACT.Exp, bias=neg_max[:, 0:1],
                                     accum_out=row_sum[:, 0:1]).then_inc(exp_ready, 1)
                nc.scalar.activation(prob[:, P:384], logit[:, P:384], ACT.Exp, bias=neg_max[:, 1:2],
                                     accum_out=row_sum[:, 1:2]).then_inc(exp_ready, 1)

            def keep_probT(n):
                act.wait_ge(t_done, n + 1)
                nc.scalar.activation(probT[:, :], turned[:, 0:384], ACT.Copy).then_inc(probT_ready, 1)

            def fox_att_hi(n):
                act.wait_ge(pv_done, n + 1)
                nc.scalar.activation(one(a_hi, n), pv_sum[:, 0:TOK], ACT.Copy).then_inc(att_hi, 1)

            act.dma_start(cols[:, :, :], norm_cols).then_inc(consts_in, 16)
            act.dma_start(hcols[:, :], head_cols).then_inc(consts_in, 16)
            act.dma_start(w_f, fox_w_f).then_inc(fox_in, 16)
            for t in range(NT):
                act.dma_start(b_f[:, t, :], fox_b_f.broadcast_to([P, FOX_HEADS])).then_inc(fox_in, 16)
            act.wait_ge(x_in, 32)
            nc.scalar.activation(gate_flat[:, 0:D], res[:, 0, :], ACT.Square,
                                 accum_out=sq_all[:, 0:1]).then_inc(sumsq_ready, 1)
            for s in range(RING):
                act.wait_ge(raw_landed[s], 16)
                nc.scalar.activation(w_hi[:, s, :], raw[:, s, :], ACT.Copy).then_inc(hi_ready, 1)
            act.wait_ge(fox_in, 48)
            nc.scalar.activation(a_hi[:, 0, :], w_f.rearrange("p k h -> p (k h)"), ACT.Copy).then_inc(wf_hi, 1)
            act.wait_ge(consts_in, 32)

            c = FIRST["fox_v"]
            norm_block(0, 0)
            for j in range(8):
                if j < 7:
                    norm_block(0, j + 1)
                split(c + j, j % RING, 1 + j // RING)
            for j in range(8, 16):
                split(c + j, j % RING, 1 + j // RING)
            act.wait_ge(f_step, 2)
            nc.scalar.activation(f_exp, f_abs, ACT.Exp).then_inc(f_exp_ready, 1)
            act.wait_ge(f_exp_ready, 1)
            nc.scalar.activation(f_ln, f_exp, ACT.Ln, bias=1.0).then_inc(f_exp_ready, 1)
            act.wait_ge(f_exp_ready, 2)
            nc.scalar.activation(f_exp[:, 0, 0:1], f_abs[:, 0, 0:1], ACT.Tanh)
            for j in range(16, 32):
                split(c + j, j % RING, 1 + j // RING)

            def fox_head(h, heads_before):
                c = FIRST["fox_qk"] + h * 4
                lap = h + (FIRST["fox_qk"] // RING + 1)
                split(c, 0, lap)
                act.wait_ge(chunk_done, c + 2)
                if heads_before >= 1:
                    act.wait_ge(s_done, h)
                nc.scalar.activation(q_head[:, :], tile_sum[0][:, 0:TOK], ACT.Copy,
                                     scale=SCALE).then_inc(q_ready, 1)
                act.wait_ge(q_ready, h + 1)
                act.sem_inc(tile_taken[0], 1)
                split(c + 1, 1, lap)
                if heads_before >= 2:
                    keep_probT(h - 2)
                split(c + 2, 2, lap)
                if heads_before >= 1:
                    exps(h - 1)
                split(c + 3, 3, lap)
                if heads_before >= 2:
                    fox_att_hi(h - 2)

            for h in range(3):
                fox_head(h, h)
            with act.Fori(3, FOX_HEADS) as h:
                fox_head(h, 3)

            def group_squares(c, g, n, sums, done):
                act.wait_ge(chunk_done, c + GROUP_CHUNKS)
                for t in range(NT):
                    if t == 1:
                        act.wait_ge(done, 2 * n + 1)
                    elif n >= 1:
                        act.wait_ge(done, 2 * n)
                    nc.scalar.activation(junk, group_bank[g][t][:, :], ACT.Square,
                                         accum_out=sums[:, t, n:n + 1]).then_inc(done, 1)

            c = FIRST["fox_out"]
            for n in range(4):
                for j in range(8):
                    k = 8 * n + j
                    if j == 7:
                        if n == 0:
                            fox_att_hi(15)
                        group_squares(c + 8 * n, n % 2, n, sq_sum, group_sq)
                    split(c + k, j % RING, (c + k) // RING + 1)
                    if n == 0 and j == 1:
                        keep_probT(14)
                    if n == 0 and j == 2:
                        exps(15)
                    if n == 0 and j == 3:
                        fox_att_hi(14)
                    if n == 0 and j == 5:
                        keep_probT(15)

            def res_squares(norm):
                for b in range(4):
                    for t in range(NT):
                        n = 8 * (norm - 1) + 2 * b + t
                        act.wait_ge(res_added, n + 1)
                        if n % 8 > 0:
                            act.wait_ge(sumsq_ready, 2 + n)
                        nc.scalar.activation(junk, res[:, t, b * GROUP_COLS:(b + 1) * GROUP_COLS], ACT.Square,
                                             accum_out=sq_sum[:, t, b:b + 1]).then_inc(sumsq_ready, 1)

            res_squares(1)
            for j in range(8):
                norm_block(1, j)

            def mlp_group(g, last):
                c = FIRST["mlp"] + g * 64
                lap = g * 16 + (FIRST["mlp"] // RING + 1)
                with act.Fori(0, 8) as i:
                    for b in range(2):
                        tile = g * 16 + (i * 2 + b)
                        c_b = c + (i * 4 + 2 * b)
                        split(c_b, 2 * b, lap + i)
                        act.wait_ge(chunk_done, c_b + 2)
                        nc.scalar.activation(relu[b], tile_sum[b][:, 0:TOK], ACT.Relu).then_inc(relu_ready, 1)
                        act.wait_ge(relu_ready, tile + 1)
                        act.sem_inc(tile_taken[b], 1)
                        nc.scalar.activation(one(a_hi, i * 2 + b), relu[b], ACT.Square).then_inc(ff_hi, 1)
                        split(c_b + 1, 2 * b + 1, lap + i)
                if not last:
                    with act.Fori(0, 8) as i:
                        splits(c + (i * 4 + 32), lap + (i + 8), range(RING))
                    return
                for n in range(4):
                    for j in range(8):
                        k = 32 + 8 * n + j
                        split(c + k, j % RING, (c + k) // RING + 1)
                    for t in range(NT):
                        act.wait_ge(ff_sum_ready, 24 + 2 * n + t + 1)
                        if 2 * n + t > 0:
                            act.wait_ge(ff_sq, 2 * n + t)
                        nc.scalar.activation(junk, group_sum[:, t, n * GROUP_COLS:(n + 1) * GROUP_COLS],
                                             ACT.Square, accum_out=sq_sum[:, t, n:n + 1]).then_inc(ff_sq, 1)

            with act.Fori(0, FF_GROUPS - 1) as g:
                mlp_group(g, False)
            mlp_group(FF_GROUPS - 1, True)
            res_squares(2)

            c = FIRST["qkv"]
            norm_block(2, 0)
            for n in range(2):
                for j in range(8):
                    k = 8 * n + j
                    if n == 0 and j < 7:
                        norm_block(2, j + 1)
                    split(c + k, j % RING, (c + k) // RING + 1)
                for t in range(NT):
                    m = 2 * n + t
                    if m >= 2:
                        act.wait_ge(vb_sums, m - 1)
                    nc.scalar.activation(gelu_a[:, t, :], group_bank[n][t][:, :], ACT.Square).then_inc(vb_sq1, 1)
                for t in range(NT):
                    m = 2 * n + t
                    act.wait_ge(vb_cube, m + 1)
                    nc.scalar.activation(gelu_a[:, t, :], gelu_b[:, t, :], ACT.Tanh,
                                         scale=GELU_SCALE).then_inc(vb_tanh, 1)
                for t in range(NT):
                    m = 2 * n + t
                    act.wait_ge(vb_gelu, m + 1)
                    nc.scalar.activation(gelu_a[:, t, :], vb[:, t, n * GROUP_COLS:(n + 1) * GROUP_COLS],
                                         ACT.Square).then_inc(vb_sq2, 1)
            with act.Fori(1, 4) as i:
                for g in range(2):
                    c_g = FIRST["qkv"] + (i * 16 + 8 * g)
                    lap = i * 4 + (FIRST["qkv"] // RING + 1 + 2 * g)
                    splits(c_g, lap, range(RING))
                    splits(c_g + 4, lap + 1, range(RING))
                    for t in range(NT):
                        m = i * 4 + (2 * g + t - 4)
                        act.wait_ge(qkv_sums, m + 1)
                        nc.scalar.activation(gelu_a[:, t, :], group_bank[g][t][:, :],
                                             ACT.Square).then_inc(qkv_sq, 1)

            def uz_chunks(base, i, b):
                return (FIRST["sgu_uz"] + base * 16 + (i * 4 + 2 * b),
                        i + (FIRST["sgu_uz"] // RING + base * 4 + 1))

            act.wait_ge(qkv_sums, 14)
            with act.Fori(0, 4) as i:
                for b in range(2):
                    g = i * 2 + b
                    c, lap = uz_chunks(0, i, b)
                    split(c, 2 * b, lap)
                    act.wait_ge(chunk_done, c + 2)
                    nc.scalar.activation(uz_a[b], tile_sum[b][:, 0:TOK], ACT.Square).then_inc(uz_sq, 1)
                    split(c + 1, 2 * b + 1, lap)
                    act.wait_ge(uz_cube, g + 1)
                    nc.scalar.activation(uz_b[b], uz_a[b], ACT.Tanh, scale=GELU_SCALE).then_inc(uz_tanh, 1)
            with act.Fori(0, 4) as i:
                for b in range(2):
                    g = i * 2 + b
                    c, lap = uz_chunks(1, i, b)
                    split(c, 2 * b, lap)
                    act.wait_ge(chunk_done, c + 2)
                    nc.scalar.activation(uz_a[b], tile_sum[b][:, 0:TOK], ACT.Tanh, scale=0.5).then_inc(zb_tanh, 1)
                    split(c + 1, 2 * b + 1, lap)
                    act.wait_ge(sgu_f, g + 1)
                    nc.scalar.activation(one(a_hi, g + 8), uz_a[b], ACT.Copy).then_inc(sgu_hi, 1)
            with act.Fori(0, 4) as i:
                for b in range(2):
                    c, lap = uz_chunks(2, i, b)
                    split(c, 2 * b, lap)
                    act.wait_ge(chunk_done, c + 2)
                    nc.scalar.activation(uz_a[b], tile_sum[b][:, 0:TOK], ACT.Tanh, scale=0.5).then_inc(za_tanh, 1)
                    split(c + 1, 2 * b + 1, lap)

            def moba_att_hi(n):
                act.wait_ge(att_f_ready, n - 15)
                nc.scalar.activation(one(a_hi, n - FOX_HEADS), att_f[:, :], ACT.Copy).then_inc(att_hi, 1)

            def gate_head(h, first):
                n = h + FOX_HEADS

                def gate_tile(u):
                    c = FIRST["gates"] + h * 8 + 2 * u
                    s = (2 * u) % RING
                    lap = h * 2 + (FIRST["gates"] // RING + 1 + u // 2)
                    split(c, s, lap)
                    act.wait_ge(chunk_done, c + 2)
                    nc.scalar.activation(one(gate, h * 4 + u), tile_sum[u % 2][:, 0:TOK], ACT.Tanh,
                                         scale=0.5).then_inc(gate_ready, 1)
                    act.wait_ge(gate_ready, h * 4 + (u + 1))
                    act.sem_inc(tile_taken[u % 2], 1)
                    split(c + 1, s + 1, lap)

                gate_tile(0)
                act.wait_ge(qk_turned, h + 1)
                nc.scalar.activation(q_head[:, :], turned[:, 0:TOK], ACT.Copy,
                                     scale=hscale[:, 0:1]).then_inc(q_ready, 1)
                if not first:
                    moba_att_hi(n - 1)
                gate_tile(1)
                gate_tile(2)
                exps(n)
                gate_tile(3)
                keep_probT(n)

            act.wait_ge(scale_made, 2)
            act.wait_ge(za_ready, 8)
            gate_head(0, True)
            with act.Fori(1, MOBA_HEADS) as h:
                gate_head(h, False)
            moba_att_hi(FOX_HEADS + MOBA_HEADS - 1)

            with act.Fori(0, 4) as i:
                splits(FIRST["proj_b"] + i * 4, i + (FIRST["proj_b"] // RING + 1), range(RING))
            with act.Fori(0, 4) as i:
                for s in range(4):
                    f = i * 4 + s
                    split(FIRST["proj_a"] + f, s, i + (FIRST["proj_a"] // RING + 1))
                    act.wait_ge(merged_f, f + 1)
                    nc.scalar.activation(one(h_hi, f), merge_s[s % 2], ACT.Copy, scale=0.5).then_inc(merged_hi, 1)
            c = FIRST["out"]
            for k in range(32 - RING):
                split(c + k, k % RING, (c + k) // RING + 1)

        @block.vector
        def _(dve):
            def rest(c, slot):
                dve.wait_ge(hi_ready, c + (RING + 1))
                nc.vector.tensor_tensor(w_lo[:, slot, :], raw[:, slot, :], w_hi[:, slot, :].bitcast(F32),
                                        ALU.subtract).then_inc(lo_ready, 1)

            def rests(c, slots):
                for s in slots:
                    rest(c + s, s)

            def norm_block(norm, j):
                n = 8 * norm + j
                dve.wait_ge(xt_hi, 2 * n + 2)
                for k in range(2):
                    kt = 2 * j + k
                    ins = nc.vector.scalar_tensor_tensor(
                        out=h_lo[:, kt, :], in0=bank[6 + n % 2][:, k * TOK:(k + 1) * TOK],
                        scalar=cols[:, norm, kt:kt + 1], in1=h_hi[:, kt, :].bitcast(F32),
                        op0=ALU.mult, op1=ALU.subtract)
                ins.then_inc(h_ready, 1)

            def soften(n, add):
                dve.wait_ge(s_done, n + 1)
                nc.vector.tensor_tensor(logit[:, :], score[:, 0:384], add[:, :], ALU.add).then_inc(logit_ready, 1)
                dve.wait_ge(logit_ready, n + 1)
                nc.vector.tensor_reduce(neg_max[:, 0:1], logit[:, 0:P], AX.X, ALU.max,
                                        negate=True).then_inc(max_ready, 1)
                nc.vector.tensor_reduce(neg_max[:, 1:2], logit[:, P:384], AX.X, ALU.max,
                                        negate=True).then_inc(max_ready, 1)

            def normalise(n):
                dve.wait_ge(exp_ready, n * 2 + 2)
                nc.vector.reciprocal(row_inv[:, :], row_sum[:, :]).then_inc(inv_ready, 1)
                dve.wait_ge(inv_ready, n + 1)
                nc.vector.tensor_scalar(prob[:, 0:P], prob[:, 0:P], row_inv[:, 0:1], None,
                                        ALU.mult).then_inc(prob_ready, 1)
                nc.vector.tensor_scalar(prob[:, P:384], prob[:, P:384], row_inv[:, 1:2], None,
                                        ALU.mult).then_inc(prob_ready, 1)

            def fox_att_lo(n):
                dve.wait_ge(att_hi, n + 1)
                nc.vector.tensor_tensor(one(a_lo, n), pv_sum[:, 0:TOK], one(a_hi, n).bitcast(F32),
                                        ALU.subtract).then_inc(att_ready, 1)

            for s in (*tile_taken, *group_taken):
                dve.sem_inc(s, 1)
            dve.wait_ge(x_in, 32)
            nc.vector.tensor_tensor_reduce(gate_flat[:, D:2 * D], res[:, 1, :], res[:, 1, :], 1.0, 0.0,
                                           ALU.mult, ALU.add, sq_all[:, 1:2]).then_inc(sumsq_ready, 1)
            for s in range(RING):
                dve.wait_ge(hi_ready, s + 1)
                nc.vector.tensor_tensor(w_lo[:, s, :], raw[:, s, :], w_hi[:, s, :].bitcast(F32),
                                        ALU.subtract).then_inc(lo_ready, 1)
            dve.wait_ge(wf_hi, 1)
            nc.vector.tensor_tensor(a_lo[:, 0, :], w_f.rearrange("p k h -> p (k h)"),
                                    a_hi[:, 0, :].bitcast(F32), ALU.subtract).then_inc(wf_ready, 1)

            def keep_v(n):
                g = n % 2
                dve.wait_ge(chunk_done, FIRST["fox_v"] + 8 * (n + 1))
                cols_n = slice(n * GROUP_COLS, (n + 1) * GROUP_COLS)
                nc.vector.tensor_copy(fox_v[:, 0, cols_n], group_bank[g][0][:, :]).then_inc(v_ready, 1)
                nc.vector.tensor_copy(fox_v[:, 1, cols_n], group_bank[g][1][:, :]).then_inc(v_ready, 1)
                dve.wait_ge(v_ready, 2 * n + 2)
                dve.sem_inc(group_taken[g], 1)

            c = FIRST["fox_v"]
            dve.wait_ge(consts_in, 32)
            norm_block(0, 0)
            for j in range(8):
                if j < 7:
                    norm_block(0, j + 1)
                rest(c + j, j % RING)
            keep_v(0)
            rests(c + 8, range(RING))
            rests(c + 12, range(RING))
            keep_v(1)
            dve.wait_ge(f_done, 1)
            nc.vector.tensor_tensor(f_z, score[:, 0:32].rearrange("p (t h) -> p t h", t=NT), b_f,
                                    ALU.add).then_inc(f_step, 1)
            dve.wait_ge(f_step, 1)
            nc.vector.scalar_tensor_tensor(out=f_abs, in0=f_z, scalar=-1.0, in1=f_z, op0=ALU.mult,
                                           op1=ALU.min).then_inc(f_step, 1)
            nc.vector.tensor_scalar(f_min, f_z, 0.0, None, ALU.min).then_inc(f_step, 1)
            dve.wait_ge(f_exp_ready, 2)
            dve.wait_ge(f_step, 3)
            nc.vector.tensor_tensor(f_log, f_min, f_ln, ALU.subtract).then_inc(f_log_ready, 1)
            rests(c + 16, range(RING))
            rests(c + 20, range(RING))
            keep_v(2)
            rests(c + 24, range(RING))
            rests(c + 28, range(RING))
            keep_v(3)
            dve.wait_ge(cum_done, 1)
            nc.vector.tensor_scalar(cum_neg, turned[0:FOX_HEADS, 0:TOK], -1.0, None, ALU.mult).then_inc(cum_ready, 1)
            nc.vector.tensor_copy(cum_cols[:, :, :],
                                  turned[:, 256:288].rearrange("p (t h) -> p t h", t=NT)).then_inc(cum_ready, 1)

            def fox_head(h, heads_before):
                c = FIRST["fox_qk"] + h * 4
                rests(c, range(2))
                if heads_before >= 1:
                    dve.wait_ge(bias_ready, h)
                    soften(h - 1, bias)
                rest(c + 2, 2)
                dve.wait_ge(chunk_done, c + 4)
                nc.vector.tensor_copy(k_head[:, :], tile_sum[1][:, 0:TOK]).then_inc(k_ready, 1)
                dve.wait_ge(k_ready, h + 1)
                dve.sem_inc(tile_taken[1], 1)
                if heads_before >= 1:
                    normalise(h - 1)
                rest(c + 3, 3)
                if heads_before >= 2:
                    fox_att_lo(h - 2)

            for h in range(3):
                fox_head(h, h)
            with dve.Fori(3, FOX_HEADS) as h:
                fox_head(h, 3)

            c = FIRST["fox_out"]
            for n in range(4):
                for j in range(8):
                    if n == 0 and j == 7:
                        fox_att_lo(15)
                    if j == 7:
                        cols_n = slice(n * GROUP_COLS, (n + 1) * GROUP_COLS)
                        dve.wait_ge(group_sq, 2 * n + 2)
                        dve.wait_ge(rowg_in, 16)
                        for t in range(NT):
                            nc.vector.tensor_tensor(group_sum[:, t, cols_n], group_bank[n % 2][t][:, :],
                                                    rowg[:, cols_n], ALU.mult).then_inc(group_gained, 1)
                        dve.wait_ge(group_gained, 2 * n + 2)
                        dve.sem_inc(group_taken[n % 2], 1)
                    rest(c + 8 * n + j, j % RING)
                    if n == 0 and j == 1:
                        dve.wait_ge(bias_ready, 16)
                        soften(15, bias)
                    if n == 0 and j == 2:
                        normalise(15)
                    if n == 0 and j == 3:
                        fox_att_lo(14)

            def post_norm(norm):
                first = 4 * (norm - 1)
                nc.vector.tensor_reduce(sq_all[:, :], sq_sum[:, :, :], AX.X, ALU.add).then_inc(mean_ready, 1)
                dve.wait_ge(rstd_ready, 2 * norm)
                for b in range(4):
                    cols_b = slice(b * GROUP_COLS, (b + 1) * GROUP_COLS)
                    for t in range(NT):
                        nc.vector.scalar_tensor_tensor(out=res[:, t, cols_b], in0=group_sum[:, t, cols_b],
                                                       scalar=rstd[:, t:t + 1], in1=res[:, t, cols_b],
                                                       op0=ALU.mult, op1=ALU.add).then_inc(res_added, 1)
                dve.wait_ge(sumsq_ready, 2 + 8 * norm)
                nc.vector.tensor_reduce(sq_all[:, :], sq_sum[:, :, :], AX.X, ALU.add).then_inc(mean_ready, 1)

            post_norm(1)
            for j in range(8):
                norm_block(1, j)

            dve.wait_ge(zeroed, 1)

            def mlp_group(g, last):
                c = FIRST["mlp"] + g * 64
                with dve.Fori(0, 8) as i:
                    for b in range(2):
                        tile = g * 16 + (i * 2 + b)
                        kt = i * 2 + b
                        c_b = c + (i * 4 + 2 * b)
                        rest(c_b, 2 * b)
                        dve.wait_ge(ff_hi, tile + 1)
                        nc.vector.tensor_tensor(relu2[b], relu[b], relu[b], ALU.mult).then_inc(relu2_ready, 1)
                        dve.wait_ge(relu2_ready, tile + 1)
                        nc.vector.tensor_tensor(one(a_lo, kt), relu2[b], one(a_hi, kt).bitcast(F32),
                                                ALU.subtract).then_inc(ff_ready, 1)
                        rest(c_b + 1, 2 * b + 1)

                def add_group(n, b):
                    cc = c + (n * 8 + 40)
                    dve.wait_ge(chunk_done, cc)
                    for t in range(NT):
                        dst = group_sum[:, t, bass.ds(n * GROUP_COLS, GROUP_COLS)]
                        nc.vector.tensor_tensor(dst, dst, group_bank[b][t][:, :], ALU.add).then_inc(ff_sum_ready, 1)
                    dve.wait_ge(ff_sum_ready, g * 8 + (n * 2 + 2))
                    dve.sem_inc(group_taken[b], 1)

                if not last:
                    with dve.Fori(0, 2) as i:
                        for b in range(2):
                            rests(c + (i * 16 + (32 + 8 * b)), range(RING))
                            rests(c + (i * 16 + (36 + 8 * b)), range(RING))
                            add_group(i * 2 + b, b)
                    return
                for n in range(4):
                    cols_n = slice(n * GROUP_COLS, (n + 1) * GROUP_COLS)
                    rests(c + 32 + 8 * n, range(RING))
                    rests(c + 36 + 8 * n, range(RING))
                    add_group(n, n % 2)
                    dve.wait_ge(rowg_in, 32)
                    for t in range(NT):
                        dve.wait_ge(ff_sq, 2 * n + t + 1)
                        nc.vector.tensor_tensor(group_sum[:, t, cols_n], group_sum[:, t, cols_n],
                                                rowg[:, cols_n], ALU.mult).then_inc(group_gained, 1)

            with dve.Fori(0, FF_GROUPS - 1) as g:
                mlp_group(g, False)
            mlp_group(FF_GROUPS - 1, True)
            dve.wait_ge(group_gained, 16)
            post_norm(2)

            c = FIRST["qkv"]
            norm_block(2, 0)
            for n in range(2):
                for j in range(8):
                    if n == 0 and j < 7:
                        norm_block(2, j + 1)
                    rest(c + 8 * n + j, j % RING)
                for t in range(NT):
                    m = 2 * n + t
                    dve.wait_ge(vb_sq1, m + 1)
                    nc.vector.tensor_scalar(gelu_b[:, t, :], gelu_a[:, t, :], GELU_CUBE, 1.0, ALU.mult,
                                            ALU.add).then_inc(vb_step, 1)
                    dve.wait_ge(vb_step, m + 1)
                    nc.vector.tensor_tensor(gelu_b[:, t, :], gelu_b[:, t, :], group_bank[n][t][:, :],
                                            ALU.mult).then_inc(vb_cube, 1)
                for t in range(NT):
                    m = 2 * n + t
                    dve.wait_ge(vb_tanh, m + 1)
                    nc.vector.scalar_tensor_tensor(out=vb[:, t, n * GROUP_COLS:(n + 1) * GROUP_COLS],
                                                   in0=gelu_a[:, t, :], scalar=1.0, in1=group_bank[n][t][:, :],
                                                   op0=ALU.add, op1=ALU.mult).then_inc(vb_gelu, 1)
                dve.wait_ge(vb_gelu, 2 * n + 2)
                dve.sem_inc(group_taken[n], 1)
                for t in range(NT):
                    m = 2 * n + t
                    dve.wait_ge(vb_sq2, m + 1)
                    nc.vector.tensor_reduce(vb_sq[:, t, 4 * n:4 * n + 4],
                                            gelu_a[:, t, :].rearrange("p (h d) -> p h d", h=4), AX.X,
                                            ALU.add).then_inc(vb_sums, 1)
            dve.wait_ge(vb_sums, 4)
            dve.sem_inc(qkv_sums, 2)
            with dve.Fori(1, 4) as i:
                for g in range(2):
                    c_g = FIRST["qkv"] + (i * 16 + 8 * g)
                    rests(c_g, range(RING))
                    rests(c_g + 4, range(RING))
                    for t in range(NT):
                        m = i * 4 + (2 * g + t - 4)
                        dve.wait_ge(qkv_sq, m + 1)
                        nc.vector.tensor_copy(qkv[:, t, bass.ds(i * 1024 + (g * 512 - 1024), GROUP_COLS)],
                                              group_bank[g][t][:, :]).then_inc(qkv_in, 1)
                        nc.vector.tensor_reduce(head_sq[:, t, bass.ds(i * 8 + (4 * g - 8), 4)],
                                                gelu_a[:, t, :].rearrange("p (h d) -> p h d", h=4), AX.X,
                                                ALU.add).then_inc(qkv_sums, 1)
                    dve.wait_ge(qkv_in, i * 4 + (2 * g + 2 - 4))
                    dve.sem_inc(group_taken[g], 1)

            with dve.Fori(0, 4) as i:
                for b in range(2):
                    g = i * 2 + b
                    c = FIRST["sgu_uz"] + (i * 4 + 2 * b)
                    rest(c, 2 * b)
                    dve.wait_ge(uz_sq, g + 1)
                    nc.vector.tensor_scalar(uz_b[b], uz_a[b], GELU_CUBE, 1.0, ALU.mult, ALU.add).then_inc(uz_step, 1)
                    dve.wait_ge(uz_step, g + 1)
                    nc.vector.tensor_tensor(uz_a[b], uz_b[b], tile_sum[b][:, 0:TOK], ALU.mult).then_inc(uz_cube, 1)
                    rest(c + 1, 2 * b + 1)
                    dve.wait_ge(uz_tanh, g + 1)
                    nc.vector.scalar_tensor_tensor(out=one(u_gelu, g), in0=uz_b[b], scalar=1.0,
                                                   in1=tile_sum[b][:, 0:TOK], op0=ALU.add,
                                                   op1=ALU.mult).then_inc(u_ready, 1)
                    dve.wait_ge(u_ready, g + 1)
                    dve.sem_inc(tile_taken[b], 1)
            dve.wait_ge(scale_made, 2)
            dve.wait_ge(sgu_in, 32)
            with dve.Fori(0, 4) as i:
                for b in range(2):
                    g = i * 2 + b
                    c = FIRST["sgu_uz"] + 16 + (i * 4 + 2 * b)
                    rest(c, 2 * b)
                    dve.wait_ge(mix_done, g + 1)
                    for t in range(NT):
                        nc.vector.scalar_tensor_tensor(out=mixed[:, t * P:(t + 1) * P],
                                                       in0=score[:, t * P:(t + 1) * P], scalar=hscale[:, 2:3],
                                                       in1=one(b_s, g), op0=ALU.mult,
                                                       op1=ALU.add).then_inc(mixed_ready, 1)
                    dve.wait_ge(zb_tanh, g + 1)
                    nc.vector.scalar_tensor_tensor(out=uz_b[b], in0=uz_a[b], scalar=1.0,
                                                   in1=tile_sum[b][:, 0:TOK], op0=ALU.add,
                                                   op1=ALU.mult).then_inc(zb_silu, 1)
                    dve.wait_ge(zb_silu, g + 1)
                    dve.sem_inc(tile_taken[b], 1)
                    nc.vector.scalar_tensor_tensor(out=uz_b[b], in0=uz_b[b], scalar=0.25, in1=one(u_gelu, g),
                                                   op0=ALU.mult, op1=ALU.mult).then_inc(zb_gated, 1)
                    dve.wait_ge(zb_gated, g + 1)
                    dve.wait_ge(mixed_ready, g * 2 + 2)
                    nc.vector.tensor_tensor(uz_a[b], uz_b[b], mixed, ALU.mult).then_inc(sgu_f, 1)
                    dve.wait_ge(sgu_hi, g + 1)
                    nc.vector.tensor_tensor(one(a_lo, g + 8), uz_a[b], one(a_hi, g + 8).bitcast(F32),
                                            ALU.subtract).then_inc(sgu_ready, 1)
                    rest(c + 1, 2 * b + 1)
            with dve.Fori(0, 4) as i:
                for b in range(2):
                    g = i * 2 + b
                    c = FIRST["sgu_uz"] + 32 + (i * 4 + 2 * b)
                    rest(c, 2 * b)
                    dve.wait_ge(za_tanh, g + 1)
                    nc.vector.scalar_tensor_tensor(out=one(za_silu, g), in0=uz_a[b], scalar=1.0,
                                                   in1=tile_sum[b][:, 0:TOK], op0=ALU.add,
                                                   op1=ALU.mult).then_inc(za_ready, 1)
                    dve.wait_ge(za_ready, g + 1)
                    dve.sem_inc(tile_taken[b], 1)
                    rest(c + 1, 2 * b + 1)

            def moba_gated(n):
                dve.wait_ge(pv_done, n + 1)
                nc.vector.scalar_tensor_tensor(out=att_f[:, :], in0=pv_sum[:, 0:TOK], scalar=0.5,
                                               in1=one(za_silu, n - FOX_HEADS), op0=ALU.mult,
                                               op1=ALU.mult).then_inc(att_f_ready, 1)

            def moba_att_lo(n):
                dve.wait_ge(att_hi, n + 1)
                dve.wait_ge(att_f_ready, n - 15)
                nc.vector.tensor_tensor(one(a_lo, n - FOX_HEADS), att_f[:, :],
                                        one(a_hi, n - FOX_HEADS).bitcast(F32),
                                        ALU.subtract).then_inc(att_ready, 1)

            def gate_head(h, first):
                n = h + FOX_HEADS
                c = FIRST["gates"] + h * 8
                rests(c, range(2))
                dve.wait_ge(q_ready, n + 1)
                nc.vector.tensor_scalar(k_head[:, :], turned[:, TOK:2 * TOK], hcols[:, 1:2], None,
                                        ALU.mult).then_inc(k_ready, 1)
                if not first:
                    moba_gated(n - 1)
                rests(c + 2 - 2, range(2, 4))
                soften(n, mask)
                if not first:
                    moba_att_lo(n - 1)
                rests(c + 4, range(2))
                normalise(n)
                rests(c + 6 - 2, range(2, 4))

            gate_head(0, True)
            with dve.Fori(1, MOBA_HEADS) as h:
                gate_head(h, False)
            moba_gated(FOX_HEADS + MOBA_HEADS - 1)
            moba_att_lo(FOX_HEADS + MOBA_HEADS - 1)

            dve.wait_ge(gate_ready, 32)
            with dve.Fori(0, 4) as i:
                for s in range(4):
                    f = i * 4 + s
                    c = FIRST["proj_b"] + f
                    dve.wait_ge(chunk_done, c + 1)
                    nc.vector.scalar_tensor_tensor(out=one(merge_b, f), in0=one(gate, f + 16), scalar=1.0,
                                                   in1=tile_sum[s % 2][:, 0:TOK], op0=ALU.add,
                                                   op1=ALU.mult).then_inc(mb_ready, 1)
                    dve.wait_ge(mb_ready, f + 1)
                    dve.sem_inc(tile_taken[s % 2], 1)
                    rest(c, s)
            with dve.Fori(0, 4) as i:
                for s in range(4):
                    f = i * 4 + s
                    c = FIRST["proj_a"] + f
                    dve.wait_ge(chunk_done, c + 1)
                    nc.vector.scalar_tensor_tensor(out=merge_t[s % 2], in0=one(gate, f), scalar=1.0,
                                                   in1=tile_sum[s % 2][:, 0:TOK], op0=ALU.add,
                                                   op1=ALU.mult).then_inc(ma_ready, 1)
                    dve.wait_ge(ma_ready, f + 1)
                    dve.sem_inc(tile_taken[s % 2], 1)
                    nc.vector.tensor_tensor(merge_s[s % 2], merge_t[s % 2], one(merge_b, f),
                                            ALU.add).then_inc(merged_f, 1)
                    rest(c, s)
                    dve.wait_ge(merged_hi, f + 1)
                    nc.vector.scalar_tensor_tensor(out=one(h_lo, f), in0=merge_s[s % 2], scalar=0.5,
                                                   in1=one(h_hi, f).bitcast(F32), op0=ALU.mult,
                                                   op1=ALU.subtract).then_inc(merged_ready, 1)
            c = FIRST["out"]
            for n in range(4):
                cols_n = slice(n * GROUP_COLS, (n + 1) * GROUP_COLS)
                for j in range(8):
                    if 8 * n + j < 32 - RING:
                        rest(c + 8 * n + j, j % RING)
                dve.wait_ge(chunk_done, c + 8 * n + 8)
                for t in range(NT):
                    nc.vector.tensor_tensor(group_sum[:, t, cols_n], group_bank[n % 2][t][:, :],
                                            res[:, t, cols_n], ALU.add).then_inc(out_ready, 1)
                dve.wait_ge(out_ready, 2 * n + 2)
                dve.sem_inc(group_taken[n % 2], 1)

        @block.gpsimd
        def _(pool):
            nc.gpsimd.memset(ident[:, :], 0.0).then_inc(consts_made, 1)
            pool.wait_ge(consts_made, 1)
            nc.gpsimd.affine_select(out=ident[:, :], in_=ident[:, :], compare_op=ALU.not_equal, fill=1.0, base=0,
                                    pattern=[[-1, P]], channel_multiplier=1).then_inc(consts_made, 1)
            nc.gpsimd.memset(half_neg[:, :], -0.5).then_inc(consts_made, 1)

            def pow_norm(n):
                nc.gpsimd.tensor_scalar(mean_sq[:, :], sq_all[:, :], 1.0 / D, EPS, ALU.mult,
                                        ALU.add).then_inc(var_ready, 1)
                pool.wait_ge(var_ready, n + 1)
                nc.gpsimd.tensor_tensor(rstd[:, :], mean_sq[:, :], half_neg[:, 0:2], ALU.pow).then_inc(rstd_ready, 1)
                pool.wait_ge(rstd_ready, n + 1)

            def scale_rows(norm):
                for j in range(8):
                    n = 8 * norm + j
                    if n >= 2:
                        pool.wait_ge(xt_done, n - 1)
                    for t in range(NT):
                        nc.gpsimd.tensor_scalar(xs[n % 2][:, t, :], res[:, t, j * 256:(j + 1) * 256],
                                                rstd[:, t:t + 1], 1.0, ALU.mult, ALU.mult).then_inc(xs_ready, 1)

            pool.wait_ge(consts_made, 3)
            pool.wait_ge(sumsq_ready, 2)
            pow_norm(0)
            scale_rows(0)

            nc.gpsimd.memset(mask[:, :], 0.0).then_inc(consts_made, 1)
            pool.wait_ge(consts_made, 4)
            for b in (0, 2):
                blk = mask[:, b * P:(b + 1) * P]
                nc.gpsimd.affine_select(out=blk, in_=blk, compare_op=ALU.is_ge, fill=NEG, base=0,
                                        pattern=[[-1, P]], channel_multiplier=1).then_inc(consts_made, 1)
            pool.wait_ge(xt_done, 8)
            nc.gpsimd.memset(tri, 1.0).then_inc(consts_made, 1)
            pool.wait_ge(consts_made, 7)
            nc.gpsimd.affine_select(out=tri, in_=tri, compare_op=ALU.is_ge, fill=0.0, base=0,
                                    pattern=[[-P, NT], [1, TOK]], channel_multiplier=-1).then_inc(tri_made, 1)
            pool.wait_ge(consts_in, 32)
            nc.gpsimd.tensor_scalar(hscale[:, 0:1], hcols[:, 0:1], SCALE, 1.0, ALU.mult,
                                    ALU.mult).then_inc(scale_made, 1)
            nc.gpsimd.tensor_scalar(hscale[:, 2:3], hcols[:, 2:3], 0.5, 1.0, ALU.mult,
                                    ALU.mult).then_inc(scale_made, 1)
            pool.dma_start(rowg[:, :], norm_rows[0:1, :].broadcast_to([P, D])).then_inc(rowg_in, 16)

            pool.wait_ge(cum_ready, 2)
            pool.dma_start(fox_scratch, cum_neg).then_inc(cum_out, 16)
            pool.wait_ge(cum_out, 16)
            pool.dma_start(cum_rows.rearrange("p h t -> p (h t)"),
                           fox_scratch.rearrange("(o h) t -> o (h t)", o=1).broadcast_to([P, FOX_HEADS * TOK])
                           ).then_inc(cum_in, 16)
            pool.wait_ge(cum_in, 16)
            pool.wait_ge(v_ready, 8)

            def stage_fox(h, first):
                if not first:
                    pool.wait_ge(logit_ready, h)
                c0, c1 = [one(cum_cols[:, t:t + 1, :].rearrange("p a h -> p h a"), h) for t in range(NT)]
                rows = one(cum_rows, h)
                nc.gpsimd.tensor_tensor(bias[:, 0:P], rows[:, 0:P], c0.broadcast_to([P, P]),
                                        ALU.add).then_inc(bias_step, 1)
                nc.gpsimd.tensor_tensor(bias[:, P:384], rows, c1.broadcast_to([P, TOK]),
                                        ALU.add).then_inc(bias_step, 1)
                pool.wait_ge(bias_step, h * 2 + 2)
                nc.gpsimd.tensor_tensor(bias[:, :], bias[:, :], mask[:, :], ALU.add).then_inc(bias_ready, 1)
                if not first:
                    pool.wait_ge(pv_done, h)
                nc.gpsimd.tensor_copy(v_head[:, :, :], fox_v[:, :, bass.ds(h * P, P)]).then_inc(v_head_ready, 1)

            stage_fox(0, True)
            with pool.Fori(1, FOX_HEADS) as h:
                stage_fox(h, False)

            pool.wait_ge(mean_ready, 1)
            pow_norm(1)
            pool.wait_ge(mean_ready, 2)
            pow_norm(2)
            scale_rows(1)
            nc.gpsimd.memset(wide[:, 0:NT * D], 0.0).then_inc(zeroed, 1)
            pool.dma_start(rowg[:, :], norm_rows[1:2, :].broadcast_to([P, D])).then_inc(rowg_in, 16)

            pool.wait_ge(mean_ready, 3)
            pool.dma_start(w_s, w_spatial).then_inc(sgu_in, 16)
            pool.dma_start(b_s.rearrange("p g t -> p (g t)"), b_spatial.broadcast_to([P, 1024])).then_inc(sgu_in, 16)
            pow_norm(3)
            pool.wait_ge(mean_ready, 4)
            pow_norm(4)
            scale_rows(2)
            pool.wait_ge(sgu_in, 32)
            nc.gpsimd.affine_select(out=w_s, in_=w_s, compare_op=ALU.is_ge, fill=0.0, base=0,
                                    pattern=[[0, 8], [1, P]], channel_multiplier=-1).then_inc(w_s_ready, 1)

            pool.wait_ge(vb_sums, 4)
            nc.gpsimd.tensor_scalar(vb_sq[:, :, :], vb_sq[:, :, :], 0.25 / P, EPS, ALU.mult,
                                    ALU.add).then_inc(hvar, 1)
            pool.wait_ge(hvar, 1)
            nc.gpsimd.tensor_tensor(vb_rstd[:, :, :].rearrange("p t h -> p (t h)"),
                                    vb_sq[:, :, :].rearrange("p t h -> p (t h)"), half_neg[:, 0:16],
                                    ALU.pow).then_inc(hr_ready, 1)
            pool.wait_ge(hr_ready, 1)

            def rows_by_head(dst, src, r, h):
                for t in range(NT):
                    s = src[:, t, bass.ds(h * P, P)]
                    c = r[:, t, bass.ds(h, 1)].broadcast_to([P, P])
                    ins = nc.gpsimd.tensor_tensor(dst[:, t, :], s, c, ALU.mult)
                return ins

            rows_by_head(vb_head, vb, vb_rstd, 0).then_inc(vb_head_ready, 1)
            with pool.Fori(1, 8) as g:
                pool.wait_ge(mixed_ready, g * 2)
                rows_by_head(vb_head, vb, vb_rstd, g).then_inc(vb_head_ready, 1)

            pool.wait_ge(qkv_sums, 14)
            nc.gpsimd.tensor_scalar(head_sq[:, :, :], head_sq[:, :, :], 1.0 / P, EPS, ALU.mult,
                                    ALU.add).then_inc(hvar, 1)
            pool.wait_ge(hvar, 2)
            nc.gpsimd.tensor_tensor(head_rstd[:, :, :].rearrange("p t h -> p (t h)"),
                                    head_sq[:, :, :].rearrange("p t h -> p (t h)"), half_neg[:, :],
                                    ALU.pow).then_inc(hr_ready, 1)
            pool.wait_ge(hr_ready, 2)

            def stage_moba(h, first):
                if not first:
                    pool.wait_ge(qk_turned, h)
                rows_by_head(qk_norm[:, 0:2, :], qkv, head_rstd, h).then_inc(qk_norm_ready, 1)
                rows_by_head(qk_norm[:, 2:4, :], qkv, head_rstd, h + 8).then_inc(qk_norm_ready, 1)
                pool.wait_ge(pv_done, h + FOX_HEADS)
                nc.gpsimd.tensor_copy(v_head[:, :, :],
                                      qkv[:, :, bass.ds(h * P + 2048, P)]).then_inc(v_head_ready, 1)

            stage_moba(0, True)
            with pool.Fori(1, MOBA_HEADS) as h:
                stage_moba(h, False)


def feature_tiles(w):
    k, f = w.shape
    return w.reshape(k // 1024, 8, P, f // P, P).transpose(3, 0, 2, 1, 4).reshape(-1, P, CHUNK)


def token_groups(w):
    k, f = w.shape
    return w.reshape(k // 256, 2, P, f // GROUP_COLS, GROUP_COLS).transpose(3, 0, 2, 1, 4).reshape(-1, P, CHUNK)


def kernel(**inputs):
    import numpy as np
    import concourse.bacc as bacc
    from concourse.bass_utils import run_bass_kernel_spmd

    a = {k: np.asarray(v) for k, v in inputs.items()}
    fox = a["fox_w_in"][0]
    w1, w2, w2nd = a["mlp_w1"][0], a["mlp_w2"][0], a["w_in_2"][0]
    q, k, v, z_a, u_b, v_b, z_b = [w2nd[:, n * 1024:(n + 1) * 1024] for n in range(7)]
    fox_q = feature_tiles(fox[:, 0:D]).reshape(FOX_HEADS, TILE_CHUNKS, P, CHUNK)
    fox_k = feature_tiles(fox[:, D:2 * D]).reshape(FOX_HEADS, TILE_CHUNKS, P, CHUNK)
    parts = [
        token_groups(fox[:, 2 * D:3 * D]),
        np.stack([fox_q, fox_k], axis=1).reshape(-1, P, CHUNK),
        token_groups(a["fox_w_out"][0]),
    ]
    for g in range(FF_GROUPS):
        parts += [feature_tiles(w1[:, g * D:(g + 1) * D]), token_groups(w2[g * D:(g + 1) * D, :])]
    parts += [token_groups(m) for m in (v_b, q, k, v)]
    parts += [feature_tiles(m) for m in (u_b, z_b, z_a, w2nd[:, 7168:], a["w_proj_b_2"][0], a["w_proj_a_2"][0])]
    parts += [token_groups(a["w_out_2"][0])]
    by_feature = lambda g: g.reshape(KT, P).T
    arrays = {
        "stream": np.concatenate(parts, axis=0),
        "x": a["x"],
        "fox_w_f": np.ascontiguousarray(fox[:, 3 * D:].reshape(KT, P, FOX_HEADS).transpose(1, 0, 2)),
        "fox_b_f": a["fox_b_f"],
        "norm_rows": np.ascontiguousarray(a["norm_g"][0][[1, 3]]),
        "norm_cols": np.ascontiguousarray(np.stack(
            [by_feature(a["norm_g"][0, 0]), by_feature(a["norm_g"][0, 2]), by_feature(a["norm_g_2"][0])], axis=1)),
        "w_spatial": np.ascontiguousarray(a["w_spatial_2"][0].transpose(2, 0, 1)),
        "b_spatial": np.ascontiguousarray(a["b_spatial_2"][0].reshape(1, 1024)),
        "head_cols": np.ascontiguousarray(np.stack(
            [a["q_norm_g_2"][0], a["k_norm_g_2"][0], a["sgu_norm_g_2"][0]], axis=1)),
    }
    nc = bacc.Bacc("TRN2", target_bir_lowering=False, num_devices=1)
    aps = [nc.dram_tensor(f"in_{name}", v.shape, mybir.dt.from_np(v.dtype), kind="ExternalInput").ap()
           for name, v in arrays.items()]
    out = nc.dram_tensor("out", (1, TOK, D), F32, kind="ExternalOutput").ap()
    build(nc, *aps, out)
    r = run_bass_kernel_spmd(nc, [{f"in_{name}": v for name, v in arrays.items()}], core_ids=[0])
    return r.results[0]["out"]
```

```python
from contextlib import ExitStack

import concourse.bass as bass
from concourse import mybir

ALU = mybir.AluOpType
ACT = mybir.ActivationFunctionType
AX = mybir.AxisListType
F32 = mybir.dt.float32
F32R = mybir.dt.float32r

P = 128
TOK = 256
NT = TOK // P
D = 2048
KT = D // P
FOX_HEADS = 16
MOBA_HEADS = 8
FF_GROUPS = 4
CHUNK = 1024
RING = 4
TILE_CHUNKS = 2
GROUP_CHUNKS = 8
GROUP_COLS = 512
EPS = 1e-6
SCALE = float(P) ** -0.5
NEG = -1e30
GELU_CUBE = 0.044715
GELU_SCALE = 0.7978845608028654
CLOCK_STEPS = (10, 12, 24)
CLOCK_STEPS_FIRST = 14

PHASES = [("fox_v", 32), ("fox_qk", 64), ("fox_out", 32), ("mlp", 256), ("qkv", 64), ("sgu_uz", 48),
          ("gates", 64), ("proj_b", 16), ("proj_a", 16), ("out", 32)]
FIRST = {}
for _name, _n in PHASES:
    FIRST[_name] = sum(n for m, n in PHASES[:len(FIRST)])
N_CHUNKS = sum(n for _, n in PHASES)
TILES_BEFORE = {"fox_qk": 0, "mlp": 32, "sgu_uz": 96, "gates": 120, "proj_b": 152, "proj_a": 168}
GROUPS_BEFORE = {"fox_v": 0, "fox_out": 4, "mlp": 8, "qkv": 24, "out": 32}


def one(ap, index):
    if isinstance(index, int):
        return ap[:, index, :]
    return ap[:, bass.ds(index, 1), :].rearrange("p a n -> p (a n)")


def build(nc, stream, x, fox_w_f, fox_b_f, norm_rows, norm_cols, w_spatial, b_spatial, head_cols, out):
    fox_scratch = nc.dram_tensor("cum_rows", (FOX_HEADS, TOK), F32, kind="Internal").ap()

    with ExitStack() as ctx:
        def sb(name, shape, dt=F32):
            return ctx.enter_context(nc.sbuf_tensor(name, shape, dt))

        def sem(name):
            return ctx.enter_context(nc.semaphore(name))

        raw = sb("raw", [P, RING, CHUNK])
        w_hi = sb("w_hi", [P, RING, CHUNK], F32R)
        w_lo = sb("w_lo", [P, RING, CHUNK], F32R)
        res = sb("res", [P, NT, D])
        h_both = sb("h_both", [P, KT, 2 * TOK], F32R)
        a_both = sb("a_both", [P, KT, 2 * TOK], F32R)
        h_hi, a_hi = [both[:, :, 0:TOK] for both in (h_both, a_both)]
        h_lo, a_lo = [both[:, :, TOK:2 * TOK] for both in (h_both, a_both)]
        wide = sb("wide", [P, 6144])
        gate = sb("gate", [P, 32, TOK])
        rowg = sb("rowg", [P, D])
        ident = sb("ident", [P, P])
        mask = sb("mask", [P, 384])
        bias = sb("bias", [P, 384])
        logit = sb("logit", [P, 384])
        prob = sb("prob", [P, 384])
        probT = sb("probT", [P, 384])
        q_head = sb("q_head", [P, TOK])
        k_head = sb("k_head", [P, TOK])
        v_head = sb("v_head", [P, NT, P])
        qk_norm = sb("qk_norm", [P, 4, P])
        att_f = bias[:, 0:TOK]
        neg_max = sb("neg_max", [P, 2])
        row_sum = sb("row_sum", [P, 2])
        row_inv = sb("row_inv", [P, 2])
        cols = sb("cols", [P, 3, KT])
        hcols = sb("hcols", [P, 3])
        hscale = sb("hscale", [P, 3])
        sq_sum = sb("sq_sum", [P, NT, 4])
        sq_all = sb("sq_all", [P, 2])
        mean_sq = sb("mean_sq", [P, 2])
        post_rstd = sb("post_rstd", [P, 2])
        rstd = sb("rstd", [P, 2])
        rstd_sq = sb("rstd_sq", [P, 2])
        rstd_rows = sb("rstd_rows", [P, TOK])
        ones = sb("ones", [P, P])
        half_neg = sb("half_neg", [P, 48])
        cum_cols = sb("cum_cols", [P, NT, FOX_HEADS])
        head_sq = sb("head_sq", [P, NT, 24])
        head_rstd = sb("head_rstd", [P, NT, 24])
        vb_sq = sb("vb_sq", [P, NT, 8])
        vb_rstd = sb("vb_rstd", [P, NT, 8])

        group_sum = wide[:, 0:NT * D].rearrange("p (t n) -> p t n", t=NT)
        qkv = wide[:, :].rearrange("p (t n) -> p t n", t=NT)
        merge_b = wide[:, 0:KT * TOK].rearrange("p (k t) -> p k t", k=KT)
        spare = wide[:, 4096:6144]
        junk = spare[:, 512:1024]
        rstd_diag = qk_norm[:, 0:2, :]
        merge_t = [spare[:, b * 256:(b + 1) * 256] for b in range(2)]
        merge_s = [spare[:, 512 + b * 256:768 + b * 256] for b in range(2)]
        w_f = spare[:, 1024:1280].rearrange("p (k h) -> p k h", k=KT)
        b_f = spare[:, 1280:1312].rearrange("p (t h) -> p t h", t=NT)
        f_z, f_abs, f_min, f_exp, f_ln, f_log = [
            spare[:, 1312 + 32 * n:1344 + 32 * n].rearrange("p (t h) -> p t h", t=NT) for n in range(6)]
        cum_neg = spare[0:FOX_HEADS, 1504:1760]
        f_rows = spare[0:FOX_HEADS, 1760:2016]
        tri = spare[:, 0:512].rearrange("p (b t) -> p b t", b=NT)
        f_zero = [a_both[:, 4 * n:4 * n + 4, :] for n in range(2)]
        f_cols = [a.rearrange("p a (b m) -> p (a b) m", b=4) for a in f_zero]
        gate_flat = gate[:, :, :].rearrange("p k t -> p (k t)")
        fox_v = gate_flat[:, 0:4096].rearrange("p (t n) -> p t n", t=NT)
        cum_rows = gate_flat[:, 4096:8192].rearrange("p (h t) -> p h t", h=FOX_HEADS)
        hidden = [gate_flat[:, b * 256:(b + 1) * 256] for b in range(2)]
        relu2 = [gate_flat[:, 512 + b * 256:768 + b * 256] for b in range(2)]
        vb = gate_flat[:, 0:2048].rearrange("p (t n) -> p t n", t=NT)
        u_gelu = gate_flat[:, 2048:4096].rearrange("p (g t) -> p g t", g=8)
        w_s = gate_flat[:, 4096:5120].rearrange("p (g t) -> p g t", g=8)
        b_s = gate_flat[:, 5120:6144].rearrange("p (g t) -> p g t", g=8)
        gelu_a = gate_flat[:, 6144:7168].rearrange("p (t n) -> p t n", t=NT)
        gelu_b = gate_flat[:, 7168:8192].rearrange("p (t n) -> p t n", t=NT)
        uz_a = [gate_flat[:, 6144 + b * 256:6400 + b * 256] for b in range(2)]
        uz_b = [gate_flat[:, 6656 + b * 256:6912 + b * 256] for b in range(2)]
        uz_x = [gate_flat[:, 7680 + b * 256:7936 + b * 256] for b in range(2)]
        mixed = gate_flat[:, 7168:7424]
        vb_head = [gate_flat[:, 7424:7680].rearrange("p (t n) -> p t n", t=NT), v_head]
        za_silu = rowg[:, :].rearrange("p (g t) -> p g t", g=8)

        bank = [ctx.enter_context(nc.psum_tensor(f"bank{n}", [P, 512], F32)) for n in range(8)]
        tile_sum = bank[0:2]
        group_bank = [bank[2:4], bank[4:6]]
        pv_sum = bank[4]
        score = bank[6]
        turned = bank[7]
        mix_bank = bank[6:8]

        def turn_bank(norm, j):
            return bank[(6, 7, 4, 5)[j % 4] if norm == 1 else 6 + j % 2]

        raw_landed = [sem(f"raw_landed{n}") for n in range(RING)]
        hi_ready = sem("hi_ready")
        lo_ready = sem("lo_ready")
        chunk_done = sem("chunk_done")
        half_group_done = sem("half_group_done")
        tile_taken = [sem("tile_taken0"), sem("tile_taken1")]
        group_taken = [sem("group_taken0"), sem("group_taken1")]
        cols_in = sem("cols_in")
        hcols_in = sem("hcols_in")
        x_in = [sem(f"x_in{n}") for n in range(4)]
        fox_in = sem("fox_in")
        rowg_in = sem("rowg_in")
        sgu_in = sem("sgu_in")
        w_s_ready = sem("w_s_ready")
        consts_made = sem("consts_made")
        tri_made = sem("tri_made")
        scale_made = sem("scale_made")
        sumsq_ready = sem("sumsq_ready")
        mean_ready = sem("mean_ready")
        var_ready = sem("var_ready")
        rstd_ready = sem("rstd_ready")
        post_var = sem("post_var")
        post_ready = sem("post_ready")
        post_mean = sem("post_mean")
        rstd_sq_ready = sem("rstd_sq_ready")
        diag_ready = sem("diag_ready")
        rows_done = sem("rows_done")
        rows_ready = sem("rows_ready")
        f_zeroed = sem("f_zeroed")
        f_rows_ready = sem("f_rows_ready")
        f_turned = sem("f_turned")
        xt_done = sem("xt_done")
        xt_hi = sem("xt_hi")
        h_ready = sem("h_ready")
        group_sq = sem("group_sq")
        group_gained = sem("group_gained")
        res_added = sem("res_added")
        wf_hi = sem("wf_hi")
        wf_ready = sem("wf_ready")
        f_done = sem("f_done")
        f_z_ready = sem("f_z_ready")
        f_step = sem("f_step")
        f_exp_ready = sem("f_exp_ready")
        f_log_ready = sem("f_log_ready")
        cum_done = sem("cum_done")
        cum_ready = sem("cum_ready")
        cum_out = sem("cum_out")
        cum_in = sem("cum_in")
        v_ready = sem("v_ready")
        q_summed = sem("q_summed")
        k_summed = sem("k_summed")
        q_ready = sem("q_ready")
        k_ready = sem("k_ready")
        bias_step = sem("bias_step")
        bias_ready = sem("bias_ready")
        v_head_ready = sem("v_head_ready")
        s_done = sem("s_done")
        logit_ready = sem("logit_ready")
        max_ready = sem("max_ready")
        exp_ready = sem("exp_ready")
        inv_ready = sem("inv_ready")
        prob_ready = sem("prob_ready")
        t_done = sem("t_done")
        probT_ready = sem("probT_ready")
        pv_done = sem("pv_done")
        att_f_ready = sem("att_f_ready")
        att_hi = sem("att_hi")
        att_ready = sem("att_ready")
        hidden_summed = sem("hidden_summed")
        relu2_ready = sem("relu2_ready")
        ff_hi = sem("ff_hi")
        ff_ready = sem("ff_ready")
        ff_sum_ready = sem("ff_sum_ready")
        ff_sq = sem("ff_sq")
        zeroed = sem("zeroed")
        vb_x = sem("vb_x")
        vb_sq1 = sem("vb_sq1")
        vb_step = sem("vb_step")
        vb_cube = sem("vb_cube")
        vb_tanh = sem("vb_tanh")
        vb_gelu = sem("vb_gelu")
        vb_sq2 = sem("vb_sq2")
        vb_sums = sem("vb_sums")
        qkv_sq = sem("qkv_sq")
        qkv_in = sem("qkv_in")
        qkv_sums = sem("qkv_sums")
        hvar = sem("hvar")
        hr_ready = sem("hr_ready")
        vb_head_ready = sem("vb_head_ready")
        mix_done = sem("mix_done")
        uz_summed = sem("uz_summed")
        uz_scaled = sem("uz_scaled")
        uz_sq = sem("uz_sq")
        uz_step = sem("uz_step")
        uz_cube = sem("uz_cube")
        uz_tanh = sem("uz_tanh")
        u_ready = sem("u_ready")
        mixed_ready = sem("mixed_ready")
        mixed_u = sem("mixed_u")
        zb_tanh = sem("zb_tanh")
        zb_silu = sem("zb_silu")
        sgu_f = sem("sgu_f")
        sgu_hi = sem("sgu_hi")
        sgu_ready = sem("sgu_ready")
        za_tanh = sem("za_tanh")
        za_ready = sem("za_ready")
        qk_norm_ready = sem("qk_norm_ready")
        qk_turned = sem("qk_turned")
        gate_summed = sem("gate_summed")
        gate_scaled = sem("gate_scaled")
        gate_ready = sem("gate_ready")
        mb_summed = sem("mb_summed")
        mb_ready = sem("mb_ready")
        ma_ready = sem("ma_ready")
        merged_f = sem("merged_f")
        merged_hi = sem("merged_hi")
        merged_ready = sem("merged_ready")
        out_ready = sem("out_ready")
        stored = sem("stored")

        block = ctx.enter_context(nc.Block())

        @block.sync
        def _(sp):
            def load(c, slot):
                sp.dma_start(raw[:, slot, :],
                             stream[bass.ds(c, 1), :, :].rearrange("a p n -> p (a n)")
                             if not isinstance(c, int) else stream[c, :, :]).then_inc(raw_landed[slot], 16)

            x_rows = x[0].rearrange("(t p) n -> p t n", p=P)
            for slot in range(RING):
                block_cols = slice(slot * GROUP_COLS, (slot + 1) * GROUP_COLS)
                sp.dma_start(res[:, :, block_cols], x_rows[:, :, block_cols]).then_inc(x_in[slot], 16)
                load(slot, slot)
            with sp.Fori(1, N_CHUNKS // RING) as j:
                for slot in range(RING):
                    sp.wait_ge(lo_ready, j * RING + (slot + 1 - RING))
                    load(j * RING + slot, slot)
            for n in range(4):
                for t in range(NT):
                    sp.wait_ge(out_ready, n * NT + t + 1)
                    cols_n = slice(n * GROUP_COLS, (n + 1) * GROUP_COLS)
                    sp.dma_start(out[0, t * P:(t + 1) * P, cols_n], group_sum[:, t, cols_n]).then_inc(stored, 16)
            sp.wait_ge(stored, 16 * 4 * NT)

        @block.tensor
        def _(pe):
            def tile_chunk_halves(c, slot, dst, k0, x_both, first, last, before={}):
                pe.wait_ge(lo_ready, c + 1)
                for k in range(8):
                    if k in before:
                        before[k]()
                    w = slice(k * P, (k + 1) * P)
                    pe.matmul(dst[:, :], w_hi[:, slot, w], x_both[:, k0 + k, :], start=first and k == 0,
                              stop=False)
                    mm = pe.matmul(dst[:, 0:TOK], w_lo[:, slot, w], x_both[:, k0 + k, 0:TOK], start=False,
                                   stop=last and k == 7)
                mm.then_inc(chunk_done, 1)

            def tile_chunk(c, slot, dst, k0, x_hi, x_lo, first, last):
                pe.wait_ge(lo_ready, c + 1)
                for k in range(8):
                    w = slice(k * P, (k + 1) * P)
                    parts = ((w_hi, x_hi), (w_hi, x_lo), (w_lo, x_hi))
                    for n, (wt, xt) in enumerate(parts):
                        mm = pe.matmul(dst[:, 0:TOK], wt[:, slot, w], xt[:, k0 + k, :],
                                       start=first and k == 0 and n == 0, stop=last and k == 7 and n == 2)
                mm.then_inc(chunk_done, 1)

            def feature_tile(c, slot, taken, b, halves=True):
                pe.wait_ge(tile_taken[b], taken + 1)
                for half in range(TILE_CHUNKS):
                    if halves:
                        tile_chunk_halves(c + half, slot + half, tile_sum[b], 8 * half, h_both, half == 0,
                                          half == 1)
                    else:
                        tile_chunk(c + half, slot + half, tile_sum[b], 8 * half, h_hi, h_lo, half == 0, half == 1)

            def group_chunk(c, slot, j, dst, x_hi, x_lo):
                pe.wait_ge(lo_ready, c + 1)
                last = j == GROUP_CHUNKS - 1
                steps = [(k, t) for k in range(2) for t in range(NT)]
                if last:
                    steps = [(k, t) for t in range(NT) for k in range(2)]
                for k, t in steps:
                    w = slice(k * GROUP_COLS, (k + 1) * GROUP_COLS)
                    tt = slice(t * P, (t + 1) * P)
                    parts = ((x_hi, w_hi), (x_lo, w_hi), (x_hi, w_lo))
                    for n, (xt, wt) in enumerate(parts):
                        mm = pe.matmul(dst[t][:, :], xt[:, 2 * j + k, tt], wt[:, slot, w],
                                       start=j == 0 and k == 0 and n == 0, stop=last and k == 1 and n == 2)
                    if last and k == 1 and t == 0:
                        mm.then_inc(half_group_done, 1)
                mm.then_inc(chunk_done, 1)

            def group_pair(c, taken, x_hi, x_lo, before={}, after={}):
                for g in range(2):
                    pe.wait_ge(group_taken[g], taken + 1)
                    for j in range(GROUP_CHUNKS):
                        if g == 0 and j in before:
                            before[j]()
                        group_chunk(c + (g * GROUP_CHUNKS + j), j % RING, j, group_bank[g], x_hi, x_lo)
                        if g == 0 and j in after:
                            after[j]()

            def keep_clock(n):
                for _ in range(n):
                    pe.transpose(tile_sum[1][:, 0:P], ident[:, :], ident[:, :])

            def turn_norm(norm, j):
                n = 8 * norm + j
                if norm == 0:
                    pe.wait_ge(x_in[j // 2], 16)
                else:
                    pe.wait_ge(res_added, 16 * (norm - 1) + 2 * j + 2)
                if norm != 1 and n >= 2:
                    pe.wait_ge(h_ready, n - 1)
                if norm == 1 and j == 2:
                    pe.wait_ge(group_taken[1], 5)
                if norm == 1 and j >= 4:
                    pe.wait_ge(h_ready, n - 3)
                for k in range(2):
                    for t in range(NT):
                        to = k * TOK + t * P
                        f0 = j * 256 + k * P
                        mm = pe.transpose(turn_bank(norm, j)[:, to:to + P], res[:, t, f0:f0 + P], ident[:, :])
                mm.then_inc(xt_done, 1)

            def norm_before(norm):
                ahead = 2 if norm == 1 else 1

                def first():
                    keep_clock(CLOCK_STEPS[norm])
                    for j in range(ahead + 1):
                        turn_norm(norm, j)
                    if norm == 0:
                        keep_clock(CLOCK_STEPS_FIRST)
                    pe.wait_ge(h_ready, 8 * norm + 1)

                def later(j):
                    def run():
                        if j + ahead < 8:
                            turn_norm(norm, j + ahead)
                        pe.wait_ge(h_ready, 8 * norm + j + 1)
                    return run
                return {0: first, **{j: later(j) for j in range(1, 8)}}

            def scores(n):
                pe.wait_ge(q_ready, n + 1)
                pe.wait_ge(k_ready, n + 1)
                pe.matmul(score[:, 0:P], q_head[:, 0:P], k_head[:, 0:P], start=True, stop=True)
                pe.matmul(score[:, P:384], q_head[:, P:TOK], k_head[:, :], start=True,
                          stop=True).then_inc(s_done, 1)

            def turn_probs(n):
                pe.wait_ge(prob_ready, 2 * n + 2)
                for b in range(3):
                    mm = pe.transpose(turned[:, b * P:(b + 1) * P], prob[:, b * P:(b + 1) * P], ident[:, :])
                mm.then_inc(t_done, 1)

            def weigh_values(n):
                pe.wait_ge(probT_ready, n + 1)
                pe.wait_ge(v_head_ready, n + 1)
                if not isinstance(n, int) or n >= 1:
                    pe.wait_ge(att_ready, n)
                pe.matmul(pv_sum[:, 0:TOK], v_head[:, 0, :], probT[:, 0:TOK], start=True, stop=False)
                pe.matmul(pv_sum[:, P:TOK], v_head[:, 1, :], probT[:, TOK:384], start=False,
                          stop=True).then_inc(pv_done, 1)

            pe.wait_ge(consts_made, 3)
            group_pair(FIRST["fox_v"], 0, h_hi, h_lo, before=norm_before(0))
            pe.wait_ge(wf_ready, 1)
            for k in range(KT):
                pe.matmul(turned[:, :], f_cols[0][:, k, :], h_both[:, k, :], start=k == 0, stop=False)
                mm = pe.matmul(turned[:, 0:TOK], f_cols[1][:, k, :], h_both[:, k, 0:TOK], start=False,
                               stop=k == KT - 1)
            mm.then_inc(f_done, 1)

            def rows_of_rstd(norm):
                pe.wait_ge(diag_ready, norm)
                for t in range(NT):
                    mm = pe.matmul(score[:, t * P:(t + 1) * P], ones[:, :], rstd_diag[:, t, :],
                                   start=True, stop=True)
                mm.then_inc(rows_done, 1)

            def turn_gates():
                pe.wait_ge(f_rows_ready, 1)
                for t in range(NT):
                    mm = pe.transpose(turned[:, 256 + 16 * t:272 + 16 * t], f_rows[:, t * P:(t + 1) * P],
                                      ident[0:FOX_HEADS, 0:FOX_HEADS])
                mm.then_inc(f_turned, 1)

            rows_of_rstd(1)
            group_pair(FIRST["fox_v"] + 16, 1, h_hi, h_lo, after={0: turn_gates})
            pe.wait_ge(f_log_ready, 1)
            pe.wait_ge(tri_made, 1)
            for b in range(NT):
                pe.matmul(turned[0:FOX_HEADS, 0:TOK], f_log[:, b, :], tri[:, b, :], start=b == 0, stop=b == 1)
            pe.matmul(turned[:, 256:272], tri[:, 0, 0:P], f_log[:, 0, :], start=True, stop=True)
            pe.matmul(turned[:, 272:288], tri[:, 0, P:TOK], f_log[:, 0, :], start=True, stop=False)
            pe.matmul(turned[:, 272:288], tri[:, 1, P:TOK], f_log[:, 1, :], start=False,
                      stop=True).then_inc(cum_done, 1)

            def fox_head(h, heads_before):
                c = FIRST["fox_qk"] + h * 4
                feature_tile(c, 0, h, 0)
                if heads_before >= 2:
                    turn_probs(h - 2)
                if heads_before >= 1:
                    scores(h - 1)
                feature_tile(c + 2, 2, h, 1)
                if heads_before >= 2:
                    weigh_values(h - 2)

            for h in range(3):
                fox_head(h, h)
            with pe.Fori(3, FOX_HEADS) as h:
                fox_head(h, 3)

            def heads_in(j):
                return lambda: pe.wait_ge(att_ready, 2 * j + 2)

            def tail(*steps):
                def run():
                    for step, n in steps:
                        step(n)
                return run

            group_pair(FIRST["fox_out"], 2, a_hi, a_lo, before={j: heads_in(j) for j in range(8)},
                       after={1: tail((turn_probs, 14), (scores, 15)), 3: tail((weigh_values, 14)),
                              4: tail((turn_probs, 15)), 5: tail((weigh_values, 15))})
            group_pair(FIRST["fox_out"] + 16, 3, a_hi, a_lo)

            def mlp_group(g, start):
                c = FIRST["mlp"] + g * 64
                with pe.Fori(start, 8) as i:
                    for b in range(2):
                        feature_tile(c + (i * 4 + 2 * b), 2 * b, g * 8 + (i + 16), b)

                def hidden_in(j):
                    return lambda: pe.wait_ge(ff_ready, g * 16 + (2 * j + 2))
                with pe.Fori(0, 2) as i:
                    group_pair(c + (i * 16 + 32), g * 2 + (i + 4), a_hi, a_lo,
                               before={j: hidden_in(j) for j in range(8)})

            before = norm_before(1)
            pe.wait_ge(tile_taken[0], 17)
            for half in range(2):
                tile_chunk_halves(FIRST["mlp"] + half, half, tile_sum[0], 8 * half, h_both, half == 0, half == 1,
                                  before={2 * j: before[4 * half + j] for j in range(4)})
            feature_tile(FIRST["mlp"] + 2, 2, 16, 1)
            mlp_group(0, 1)
            with pe.Fori(1, FF_GROUPS) as g:
                mlp_group(g, 0)

            group_pair(FIRST["qkv"], 12, h_hi, h_lo, before=norm_before(2))
            rows_of_rstd(3)
            with pe.Fori(1, 4) as i:
                group_pair(FIRST["qkv"] + i * 16, i + 12, h_hi, h_lo)

            with pe.Fori(0, 4) as i:
                for b in range(2):
                    feature_tile(FIRST["sgu_uz"] + (i * 4 + 2 * b), 2 * b,
                                 i + TILES_BEFORE["sgu_uz"] // 2, b)
            with pe.Fori(0, 4) as i:
                for b in range(2):
                    pe.wait_ge(w_s_ready, 1)
                    pe.wait_ge(vb_head_ready, i * 2 + (b + 1))
                    for t in range(NT):
                        mm = pe.matmul(mix_bank[b][:, t * P:(t + 1) * P], vb_head[b][:, t, :], one(w_s, i * 2 + b),
                                       start=True, stop=True)
                    mm.then_inc(mix_done, 1)
                    feature_tile(FIRST["sgu_uz"] + 16 + (i * 4 + 2 * b), 2 * b,
                                 i + (TILES_BEFORE["sgu_uz"] // 2 + 4), b, halves=False)
            with pe.Fori(0, 4) as i:
                for b in range(2):
                    feature_tile(FIRST["sgu_uz"] + 32 + (i * 4 + 2 * b), 2 * b,
                                 i + (TILES_BEFORE["sgu_uz"] // 2 + 8), b)

            def gate_head(h, first):
                c = FIRST["gates"] + h * 8
                n = h + FOX_HEADS
                feature_tile(c, 0, h * 2 + TILES_BEFORE["gates"] // 2, 0)
                if not first:
                    weigh_values(n - 1)
                pe.wait_ge(qk_norm_ready, h * 2 + 2)
                for b in range(4):
                    mm = pe.transpose(turned[:, b * P:(b + 1) * P], qk_norm[:, b, :], ident[:, :])
                mm.then_inc(qk_turned, 1)
                feature_tile(c + 2, 2, h * 2 + TILES_BEFORE["gates"] // 2, 1)
                scores(n)
                feature_tile(c + 4, 0, h * 2 + (TILES_BEFORE["gates"] // 2 + 1), 0)
                feature_tile(c + 6, 2, h * 2 + (TILES_BEFORE["gates"] // 2 + 1), 1)
                turn_probs(n)

            gate_head(0, True)
            with pe.Fori(1, MOBA_HEADS) as h:
                gate_head(h, False)

            def project(name, k0):
                def lap(i, after={}):
                    for s in range(4):
                        pe.wait_ge(tile_taken[s % 2], i * 2 + (TILES_BEFORE[name] // 2 + s // 2 + 1))
                        if name == "proj_b":
                            tile_chunk_halves(FIRST[name] + (i * 4 + s), s, tile_sum[s % 2], k0, a_both, True,
                                              True)
                        else:
                            tile_chunk(FIRST[name] + (i * 4 + s), s, tile_sum[s % 2], k0, a_hi, a_lo, True,
                                       True)
                        if s in after:
                            after[s]()
                if name == "proj_b":
                    lap(0, {1: lambda: weigh_values(FOX_HEADS + MOBA_HEADS - 1)})
                    with pe.Fori(1, 4) as i:
                        lap(i)
                else:
                    with pe.Fori(0, 4) as i:
                        lap(i)

            pe.wait_ge(sgu_ready, 8)
            project("proj_b", 8)
            pe.wait_ge(att_ready, FOX_HEADS + MOBA_HEADS)
            project("proj_a", 0)

            def merged_in(j):
                return lambda: pe.wait_ge(merged_ready, 2 * j + 2)

            group_pair(FIRST["out"], 16, h_hi, h_lo, before={j: merged_in(j) for j in range(8)})
            group_pair(FIRST["out"] + 16, 17, h_hi, h_lo)

        @block.scalar
        def _(act):
            def split(c, slot, lap):
                act.wait_ge(chunk_done, c + 1)
                act.wait_ge(raw_landed[slot], lap * 16 + 16)
                nc.scalar.activation(w_hi[:, slot, :], raw[:, slot, :], ACT.Copy).then_inc(hi_ready, 1)

            def splits(c, lap, slots):
                for s in slots:
                    split(c + s, s, lap)

            def norm_block(norm, j):
                n = 8 * norm + j
                act.wait_ge(xt_done, n + 1)
                for k in range(2):
                    kt = 2 * j + k
                    nc.scalar.activation(h_hi[:, kt, :], turn_bank(norm, j)[:, k * TOK:(k + 1) * TOK], ACT.Copy,
                                         scale=cols[:, norm, kt:kt + 1]).then_inc(xt_hi, 1)

            def exps(n):
                act.wait_ge(max_ready, n * 2 + 2)
                nc.scalar.activation(prob[:, 0:P], logit[:, 0:P], ACT.Exp, bias=neg_max[:, 0:1],
                                     accum_out=row_sum[:, 0:1]).then_inc(exp_ready, 1)
                nc.scalar.activation(prob[:, P:384], logit[:, P:384], ACT.Exp, bias=neg_max[:, 1:2],
                                     accum_out=row_sum[:, 1:2]).then_inc(exp_ready, 1)

            def keep_probT(n):
                act.wait_ge(t_done, n + 1)
                nc.scalar.activation(probT[:, :], turned[:, 0:384], ACT.Copy).then_inc(probT_ready, 1)

            def fox_att_hi(n):
                act.wait_ge(pv_done, n + 1)
                nc.scalar.activation(one(a_hi, n), pv_sum[:, 0:TOK], ACT.Copy).then_inc(att_hi, 1)

            act.wait_ge(consts_made, 1)
            nc.scalar.activation(sq_all[:, 0:1], half_neg[:, 0:1], ACT.Copy)
            act.dma_start(cols[:, :, :], norm_cols).then_inc(cols_in, 16)
            act.dma_start(hcols[:, :], head_cols).then_inc(hcols_in, 16)
            act.dma_start(w_f, fox_w_f).then_inc(fox_in, 16)
            for t in range(NT):
                act.dma_start(b_f[:, t, :], fox_b_f.broadcast_to([P, FOX_HEADS])).then_inc(fox_in, 16)

            def res_square(norm, n):
                b, t = n // 2, n % 2
                if norm > 0:
                    act.wait_ge(res_added, 16 * (norm - 1) + 4 * b + 4)
                if n > 0:
                    act.wait_ge(sumsq_ready, 8 * norm + n)
                nc.scalar.activation(junk, res[:, t, b * GROUP_COLS:(b + 1) * GROUP_COLS], ACT.Square,
                                     accum_out=sq_sum[:, t, b:b + 1]).then_inc(sumsq_ready, 1)

            def first_split(s):
                act.wait_ge(raw_landed[s], 16)
                nc.scalar.activation(w_hi[:, s, :], raw[:, s, :], ACT.Copy).then_inc(hi_ready, 1)

            c = FIRST["fox_v"]
            act.wait_ge(cols_in, 16)
            norm_block(0, 0)
            first_split(0)
            norm_block(0, 1)
            first_split(1)
            norm_block(0, 2)
            first_split(2)
            first_split(3)
            for j in range(8):
                if j + 3 < 8:
                    norm_block(0, j + 3)
                split(c + j, j % RING, 1 + j // RING)
                if j == 0:
                    act.wait_ge(fox_in, 48)
                    act.wait_ge(f_zeroed, 2)
                    nc.scalar.activation(f_cols[0][:, :, 0:FOX_HEADS], w_f, ACT.Copy).then_inc(wf_hi, 1)
                if 3 <= j < 7:
                    res_square(0, 2 * (j - 3))
                    res_square(0, 2 * (j - 3) + 1)
            for j in range(8, 17):
                split(c + j, j % RING, 1 + j // RING)
            act.wait_ge(f_step, 2)
            nc.scalar.activation(f_exp, f_abs, ACT.Exp).then_inc(f_exp_ready, 1)
            act.wait_ge(f_exp_ready, 1)
            nc.scalar.activation(f_ln, f_exp, ACT.Ln, bias=1.0).then_inc(f_exp_ready, 1)
            act.wait_ge(f_exp_ready, 2)
            nc.scalar.activation(f_exp[:, 0, 0:1], f_abs[:, 0, 0:1], ACT.Tanh)
            for j in range(17, 32):
                split(c + j, j % RING, 1 + j // RING)

            def fox_head(h, heads_before):
                c = FIRST["fox_qk"] + h * 4
                lap = h + (FIRST["fox_qk"] // RING + 1)
                split(c, 0, lap)
                split(c + 1, 1, lap)
                if heads_before >= 2:
                    keep_probT(h - 2)
                split(c + 2, 2, lap)
                if heads_before >= 1:
                    exps(h - 1)
                split(c + 3, 3, lap)
                if heads_before >= 2:
                    fox_att_hi(h - 2)

            for h in range(3):
                fox_head(h, h)
            with act.Fori(3, FOX_HEADS) as h:
                fox_head(h, 3)

            def group_squares(c, g, n, sums, done):
                act.wait_ge(half_group_done, GROUPS_BEFORE["fox_out"] + n + 1)
                for t in range(NT):
                    if t == 1:
                        act.wait_ge(chunk_done, c + GROUP_CHUNKS)
                    if t == 1:
                        act.wait_ge(done, 2 * n + 1)
                    elif n >= 1:
                        act.wait_ge(done, 2 * n)
                    nc.scalar.activation(junk, group_bank[g][t][:, :], ACT.Square,
                                         accum_out=sums[:, t, n:n + 1]).then_inc(done, 1)

            c = FIRST["fox_out"]
            for n in range(4):
                for j in range(8):
                    k = 8 * n + j
                    if j == 7:
                        group_squares(c + 8 * n, n % 2, n, sq_sum, group_sq)
                    split(c + k, j % RING, (c + k) // RING + 1)
                    if n == 0 and j == 1:
                        keep_probT(14)
                    if n == 0 and j == 2:
                        exps(15)
                    if n == 0 and j == 3:
                        fox_att_hi(14)
                    if n == 0 and j == 4:
                        keep_probT(15)
                    if n == 0 and j == 5:
                        fox_att_hi(15)

            for j in range(8):
                norm_block(1, j)
                res_square(1, j)

            def mlp_tiles(g, i):
                c = FIRST["mlp"] + g * 64
                lap = g * 16 + (FIRST["mlp"] // RING + 1)
                for b in range(2):
                    tile = g * 16 + (i * 2 + b)
                    c_b = c + (i * 4 + 2 * b)
                    split(c_b, 2 * b, lap + i)
                    act.wait_ge(relu2_ready, tile + 1)
                    nc.scalar.activation(one(a_hi, i * 2 + b), relu2[b], ACT.Copy).then_inc(ff_hi, 1)
                    split(c_b + 1, 2 * b + 1, lap + i)

            def mlp_group(g, start, last):
                c = FIRST["mlp"] + g * 64
                lap = g * 16 + (FIRST["mlp"] // RING + 1)
                with act.Fori(start, 8) as i:
                    mlp_tiles(g, i)
                if not last:
                    with act.Fori(0, 8) as i:
                        splits(c + (i * 4 + 32), lap + (i + 8), range(RING))
                    return
                for n in range(4):
                    for j in range(7):
                        k = 32 + 8 * n + j
                        split(c + k, j % RING, (c + k) // RING + 1)
                    for t in range(NT):
                        act.wait_ge(ff_sum_ready, 24 + 2 * n + t + 1)
                        if 2 * n + t > 0:
                            act.wait_ge(ff_sq, 2 * n + t)
                        nc.scalar.activation(junk, group_sum[:, t, n * GROUP_COLS:(n + 1) * GROUP_COLS],
                                             ACT.Square, accum_out=sq_sum[:, t, n:n + 1]).then_inc(ff_sq, 1)
                    k = 32 + 8 * n + 7
                    split(c + k, 3, (c + k) // RING + 1)

            mlp_tiles(0, 0)
            mlp_group(0, 1, False)
            with act.Fori(1, FF_GROUPS - 1) as g:
                mlp_group(g, 0, False)
            mlp_group(FF_GROUPS - 1, 0, True)

            c = FIRST["qkv"]
            norm_block(2, 0)
            norm_block(2, 1)
            for n in range(2):
                def split_next(j):
                    split(c + 8 * n + j, j % RING, (c + 8 * n + j) // RING + 1)

                for j in range(2 * n, 8):
                    if n == 0 and j + 2 < 8:
                        norm_block(2, j + 2)
                    split_next(j)
                    if n == 0 and 2 <= j < 6:
                        res_square(2, 2 * (j - 2))
                        res_square(2, 2 * (j - 2) + 1)
                act.wait_ge(rstd_ready, 3)
                for t in range(NT):
                    m = 2 * n + t
                    cols_n = slice(n * GROUP_COLS, (n + 1) * GROUP_COLS)
                    nc.scalar.activation(vb[:, t, cols_n], group_bank[n][t][:, :], ACT.Copy,
                                         scale=rstd[:, t:t + 1]).then_inc(vb_x, 1)
                    if m >= 2:
                        act.wait_ge(vb_sums, m - 1)
                    nc.scalar.activation(gelu_a[:, t, :], group_bank[n][t][:, :], ACT.Square,
                                         scale=rstd[:, t:t + 1]).then_inc(vb_sq1, 1)
                act.wait_ge(vb_sq1, 2 * n + 2)
                act.sem_inc(group_taken[n], 1)
                if n == 0:
                    split_next(8)
                for t in range(NT):
                    m = 2 * n + t
                    act.wait_ge(vb_cube, m + 1)
                    nc.scalar.activation(gelu_a[:, t, :], gelu_b[:, t, :], ACT.Tanh,
                                         scale=GELU_SCALE).then_inc(vb_tanh, 1)
                if n == 0:
                    split_next(9)
                for t in range(NT):
                    m = 2 * n + t
                    act.wait_ge(vb_gelu, m + 1)
                    nc.scalar.activation(gelu_a[:, t, :], vb[:, t, n * GROUP_COLS:(n + 1) * GROUP_COLS],
                                         ACT.Square).then_inc(vb_sq2, 1)
            with act.Fori(1, 4) as i:
                for g in range(2):
                    c_g = FIRST["qkv"] + (i * 16 + 8 * g)
                    lap = i * 4 + (FIRST["qkv"] // RING + 1 + 2 * g)
                    splits(c_g, lap, range(RING))
                    splits(c_g + 4, lap + 1, range(RING))
                    for t in range(NT):
                        m = i * 4 + (2 * g + t - 4)
                        act.wait_ge(qkv_sums, m + 1)
                        nc.scalar.activation(gelu_a[:, t, :], group_bank[g][t][:, :], ACT.Square,
                                             scale=rstd[:, t:t + 1]).then_inc(qkv_sq, 1)

            def uz_chunks(base, i, b):
                return (FIRST["sgu_uz"] + base * 16 + (i * 4 + 2 * b),
                        i + (FIRST["sgu_uz"] // RING + base * 4 + 1))

            act.wait_ge(qkv_sums, 14)
            with act.Fori(0, 4) as i:
                for b in range(2):
                    g = i * 2 + b
                    c, lap = uz_chunks(0, i, b)
                    split(c, 2 * b, lap)
                    act.wait_ge(uz_scaled, g + 1)
                    nc.scalar.activation(uz_a[b], uz_x[b], ACT.Square).then_inc(uz_sq, 1)
                    split(c + 1, 2 * b + 1, lap)
                    act.wait_ge(uz_cube, g + 1)
                    nc.scalar.activation(uz_b[b], uz_a[b], ACT.Tanh, scale=GELU_SCALE).then_inc(uz_tanh, 1)
            with act.Fori(0, 4) as i:
                for b in range(2):
                    g = i * 2 + b
                    c, lap = uz_chunks(1, i, b)
                    split(c, 2 * b, lap)
                    act.wait_ge(uz_scaled, g + 9)
                    nc.scalar.activation(uz_a[b], uz_x[b], ACT.Tanh, scale=0.5).then_inc(zb_tanh, 1)
                    split(c + 1, 2 * b + 1, lap)
                    act.wait_ge(sgu_f, g + 1)
                    nc.scalar.activation(one(a_hi, g + 8), uz_a[b], ACT.Copy).then_inc(sgu_hi, 1)
            with act.Fori(0, 4) as i:
                for b in range(2):
                    g = i * 2 + b
                    c, lap = uz_chunks(2, i, b)
                    split(c, 2 * b, lap)
                    act.wait_ge(uz_scaled, g + 17)
                    nc.scalar.activation(uz_a[b], uz_x[b], ACT.Tanh, scale=0.5).then_inc(za_tanh, 1)
                    split(c + 1, 2 * b + 1, lap)

            def moba_att_hi(n):
                act.wait_ge(att_f_ready, n - 15)
                nc.scalar.activation(one(a_hi, n - FOX_HEADS), att_f[:, :], ACT.Copy).then_inc(att_hi, 1)

            def gate_head(h, first):
                n = h + FOX_HEADS

                def gate_tile(u, within=None):
                    c = FIRST["gates"] + h * 8 + 2 * u
                    s = (2 * u) % RING
                    lap = h * 2 + (FIRST["gates"] // RING + 1 + u // 2)
                    split(c, s, lap)
                    if within is not None:
                        within(n)
                    split(c + 1, s + 1, lap)
                    act.wait_ge(gate_scaled, h * 4 + (u + 1))
                    nc.scalar.activation(one(gate, h * 4 + u), one(gate, h * 4 + u), ACT.Tanh,
                                         scale=0.5).then_inc(gate_ready, 1)

                gate_tile(0)
                act.wait_ge(qk_turned, h + 1)
                nc.scalar.activation(q_head[:, :], turned[:, 0:TOK], ACT.Copy,
                                     scale=hscale[:, 0:1]).then_inc(q_ready, 1)
                if not first:
                    moba_att_hi(n - 1)
                gate_tile(1)
                gate_tile(2, exps)
                gate_tile(3)
                keep_probT(n)

            act.wait_ge(scale_made, 2)
            gate_head(0, True)
            with act.Fori(1, MOBA_HEADS) as h:
                gate_head(h, False)

            splits(FIRST["proj_b"], FIRST["proj_b"] // RING + 1, range(2))
            moba_att_hi(FOX_HEADS + MOBA_HEADS - 1)
            splits(FIRST["proj_b"], FIRST["proj_b"] // RING + 1, range(2, RING))
            with act.Fori(1, 4) as i:
                splits(FIRST["proj_b"] + i * 4, i + (FIRST["proj_b"] // RING + 1), range(RING))
            with act.Fori(0, 4) as i:
                for s in range(4):
                    f = i * 4 + s
                    split(FIRST["proj_a"] + f, s, i + (FIRST["proj_a"] // RING + 1))
                    act.wait_ge(merged_f, f + 1)
                    nc.scalar.activation(one(h_hi, f), merge_s[s % 2], ACT.Copy, scale=0.5).then_inc(merged_hi, 1)
            c = FIRST["out"]
            for k in range(32 - RING):
                split(c + k, k % RING, (c + k) // RING + 1)

        @block.vector
        def _(dve):
            def rest(c, slot):
                dve.wait_ge(hi_ready, c + (RING + 1))
                nc.vector.tensor_tensor(w_lo[:, slot, :], raw[:, slot, :], w_hi[:, slot, :].bitcast(F32),
                                        ALU.subtract).then_inc(lo_ready, 1)

            def rests(c, slots):
                for s in slots:
                    rest(c + s, s)

            def norm_block(norm, j):
                n = 8 * norm + j
                dve.wait_ge(xt_hi, 2 * n + 2)
                for k in range(2):
                    kt = 2 * j + k
                    ins = nc.vector.scalar_tensor_tensor(
                        out=h_lo[:, kt, :], in0=turn_bank(norm, j)[:, k * TOK:(k + 1) * TOK],
                        scalar=cols[:, norm, kt:kt + 1], in1=h_hi[:, kt, :].bitcast(F32),
                        op0=ALU.mult, op1=ALU.subtract)
                ins.then_inc(h_ready, 1)

            def soften(n, add):
                dve.wait_ge(s_done, n + 1)
                nc.vector.tensor_tensor(logit[:, :], score[:, 0:384], add[:, :], ALU.add).then_inc(logit_ready, 1)
                dve.wait_ge(logit_ready, n + 1)
                nc.vector.tensor_reduce(neg_max[:, 0:1], logit[:, 0:P], AX.X, ALU.max,
                                        negate=True).then_inc(max_ready, 1)
                nc.vector.tensor_reduce(neg_max[:, 1:2], logit[:, P:384], AX.X, ALU.max,
                                        negate=True).then_inc(max_ready, 1)

            def normalise(n):
                dve.wait_ge(exp_ready, n * 2 + 2)
                nc.vector.reciprocal(row_inv[:, :], row_sum[:, :]).then_inc(inv_ready, 1)
                dve.wait_ge(inv_ready, n + 1)
                nc.vector.tensor_scalar(prob[:, 0:P], prob[:, 0:P], row_inv[:, 0:1], None,
                                        ALU.mult).then_inc(prob_ready, 1)
                nc.vector.tensor_scalar(prob[:, P:384], prob[:, P:384], row_inv[:, 1:2], None,
                                        ALU.mult).then_inc(prob_ready, 1)

            def fox_att_lo(n):
                dve.wait_ge(att_hi, n + 1)
                nc.vector.tensor_tensor(one(a_lo, n), pv_sum[:, 0:TOK], one(a_hi, n).bitcast(F32),
                                        ALU.subtract).then_inc(att_ready, 1)

            def add_halves(dst, bank_rows):
                return nc.vector.tensor_reduce(dst, bank_rows[:, :].rearrange("p (s t) -> p t s", s=2), AX.X,
                                               ALU.add)

            for s in (*tile_taken, *group_taken):
                dve.sem_inc(s, 1)

            def first_rest(s):
                dve.wait_ge(hi_ready, s + 1)
                nc.vector.tensor_tensor(w_lo[:, s, :], raw[:, s, :], w_hi[:, s, :].bitcast(F32),
                                        ALU.subtract).then_inc(lo_ready, 1)

            def scale_of_rows(norm):
                dve.wait_ge(sumsq_ready, 8 * norm + 8)
                nc.vector.tensor_reduce(sq_all[:, :], sq_sum[:, :, :], AX.X, ALU.add).then_inc(mean_ready, 1)

            def diagonal(norm):
                dve.wait_ge(rstd_ready, norm)
                for t in range(NT):
                    ins = nc.vector.tensor_scalar(rstd_diag[:, t, :], ident[:, :], rstd[:, t:t + 1], None, ALU.mult)
                ins.then_inc(diag_ready, 1 if norm == 1 else 2)

            def keep_rows(n):
                dve.wait_ge(rows_done, n)
                nc.vector.tensor_copy(rstd_rows[:, :], score[:, 0:TOK]).then_inc(rows_ready, 1)

            def keep_v(n):
                g = n % 2
                dve.wait_ge(chunk_done, FIRST["fox_v"] + 8 * (n + 1))
                cols_n = slice(n * GROUP_COLS, (n + 1) * GROUP_COLS)
                for t in range(NT):
                    nc.vector.tensor_scalar(fox_v[:, t, cols_n], group_bank[g][t][:, :], rstd[:, t:t + 1], None,
                                            ALU.mult).then_inc(v_ready, 1)
                dve.wait_ge(v_ready, 2 * n + 2)
                dve.sem_inc(group_taken[g], 1)

            c = FIRST["fox_v"]
            dve.wait_ge(cols_in, 16)
            norm_block(0, 0)
            first_rest(0)
            norm_block(0, 1)
            first_rest(1)
            norm_block(0, 2)
            first_rest(2)
            first_rest(3)
            for j in range(8):
                if j + 3 < 8:
                    norm_block(0, j + 3)
                rest(c + j, j % RING)
                if j == 1:
                    dve.wait_ge(wf_hi, 1)
                    dve.wait_ge(fox_in, 48)
                    nc.vector.tensor_tensor(f_cols[1][:, :, 0:FOX_HEADS], w_f,
                                            f_cols[0][:, :, 0:FOX_HEADS].bitcast(F32),
                                            ALU.subtract).then_inc(wf_ready, 1)
            scale_of_rows(0)
            diagonal(1)
            keep_v(0)
            rests(c + 8, range(RING))
            rests(c + 12, range(RING))
            keep_v(1)
            dve.wait_ge(f_done, 1)
            add_halves(f_rows, turned[0:FOX_HEADS, :]).then_inc(f_rows_ready, 1)
            keep_rows(1)
            rest(c + 16, 0)
            dve.wait_ge(f_turned, 1)
            for t in range(NT):
                nc.vector.scalar_tensor_tensor(out=f_z[:, t, :], in0=turned[:, 256 + 16 * t:272 + 16 * t],
                                               scalar=rstd[:, t:t + 1], in1=b_f[:, t, :], op0=ALU.mult,
                                               op1=ALU.add).then_inc(f_z_ready, 1)
            dve.wait_ge(f_z_ready, 2)
            nc.vector.scalar_tensor_tensor(out=f_abs, in0=f_z, scalar=-1.0, in1=f_z, op0=ALU.mult,
                                           op1=ALU.min).then_inc(f_step, 1)
            nc.vector.tensor_scalar(f_min, f_z, 0.0, None, ALU.min).then_inc(f_step, 1)
            dve.wait_ge(f_exp_ready, 2)
            dve.wait_ge(f_step, 2)
            nc.vector.tensor_tensor(f_log, f_min, f_ln, ALU.subtract).then_inc(f_log_ready, 1)
            rests(c + 16, range(1, RING))
            rests(c + 20, range(RING))
            keep_v(2)
            rests(c + 24, range(RING))
            rests(c + 28, range(RING))
            keep_v(3)
            dve.wait_ge(cum_done, 1)
            nc.vector.tensor_scalar(cum_neg, turned[0:FOX_HEADS, 0:TOK], -1.0, None, ALU.mult).then_inc(cum_ready, 1)
            nc.vector.tensor_copy(cum_cols[:, :, :],
                                  turned[:, 256:288].rearrange("p (t h) -> p t h", t=NT)).then_inc(cum_ready, 1)

            def fox_head(h, heads_before):
                c = FIRST["fox_qk"] + h * 4
                rest(c, 0)
                dve.wait_ge(chunk_done, c + 2)
                if heads_before >= 1:
                    dve.wait_ge(s_done, h)
                add_halves(q_head[:, :], tile_sum[0]).then_inc(q_summed, 1)
                dve.wait_ge(q_summed, h + 1)
                dve.sem_inc(tile_taken[0], 1)
                nc.vector.scalar_tensor_tensor(out=q_head[:, :], in0=q_head[:, :], scalar=SCALE,
                                               in1=rstd_rows[:, :], op0=ALU.mult, op1=ALU.mult).then_inc(q_ready, 1)
                rest(c + 1, 1)
                if heads_before >= 1:
                    dve.wait_ge(bias_ready, h)
                    soften(h - 1, bias)
                rest(c + 2, 2)
                dve.wait_ge(chunk_done, c + 4)
                add_halves(k_head[:, :], tile_sum[1]).then_inc(k_summed, 1)
                dve.wait_ge(k_summed, h + 1)
                dve.sem_inc(tile_taken[1], 1)
                nc.vector.tensor_tensor(k_head[:, :], k_head[:, :], rstd_rows[:, :], ALU.mult).then_inc(k_ready, 1)
                if heads_before >= 1:
                    normalise(h - 1)
                rest(c + 3, 3)
                if heads_before >= 2:
                    fox_att_lo(h - 2)

            dve.wait_ge(rows_ready, 1)
            for h in range(3):
                fox_head(h, h)
            with dve.Fori(3, FOX_HEADS) as h:
                fox_head(h, 3)

            def total_squares():
                nc.vector.tensor_reduce(sq_all[:, :], sq_sum[:, :, :], AX.X, ALU.add).then_inc(post_mean, 1)

            c = FIRST["fox_out"]
            for n in range(4):
                for j in range(8):
                    if j == 7:
                        cols_n = slice(n * GROUP_COLS, (n + 1) * GROUP_COLS)
                        dve.wait_ge(rowg_in, 16)
                        for t in range(NT):
                            dve.wait_ge(group_sq, 2 * n + t + 1)
                            if n == 3 and t == 1:
                                total_squares()
                            nc.vector.tensor_tensor(group_sum[:, t, cols_n], group_bank[n % 2][t][:, :],
                                                    rowg[:, cols_n], ALU.mult).then_inc(group_gained, 1)
                        dve.wait_ge(group_gained, 2 * n + 2)
                        dve.sem_inc(group_taken[n % 2], 1)
                    if 8 * n + j < 31:
                        rest(c + 8 * n + j, j % RING)
                    if n == 0 and j == 1:
                        dve.wait_ge(bias_ready, 16)
                        soften(15, bias)
                    if n == 0 and j == 2:
                        normalise(15)
                    if n == 0 and j == 3:
                        fox_att_lo(14)
                    if n == 0 and j == 5:
                        fox_att_lo(15)

            def add_block(norm, j):
                cols_j = slice(j * 256, (j + 1) * 256)
                for t in range(NT):
                    nc.vector.scalar_tensor_tensor(out=res[:, t, cols_j], in0=group_sum[:, t, cols_j],
                                                   scalar=post_rstd[:, t:t + 1], in1=res[:, t, cols_j],
                                                   op0=ALU.mult, op1=ALU.add).then_inc(res_added, 1)

            dve.wait_ge(post_ready, 1)
            for j in range(3):
                add_block(1, j)
            for j in range(8):
                norm_block(1, j)
                if j + 3 < 8:
                    add_block(1, j + 3)
            rest(c + 31, 3)

            def mlp_tiles(g, i):
                c = FIRST["mlp"] + g * 64
                for b in range(2):
                    tile = g * 16 + (i * 2 + b)
                    kt = i * 2 + b
                    c_b = c + (i * 4 + 2 * b)
                    rest(c_b, 2 * b)
                    dve.wait_ge(chunk_done, c_b + 2)
                    add_halves(hidden[b], tile_sum[b]).then_inc(hidden_summed, 1)
                    dve.wait_ge(hidden_summed, tile + 1)
                    dve.sem_inc(tile_taken[b], 1)
                    nc.vector.scalar_tensor_tensor(out=relu2[b], in0=hidden[b], scalar=0.0, in1=hidden[b],
                                                   op0=ALU.max, op1=ALU.mult).then_inc(relu2_ready, 1)
                    dve.wait_ge(ff_hi, tile + 1)
                    nc.vector.tensor_tensor(one(a_lo, kt), relu2[b], one(a_hi, kt).bitcast(F32),
                                            ALU.subtract).then_inc(ff_ready, 1)
                    rest(c_b + 1, 2 * b + 1)

            def mlp_group(g, start, last):
                c = FIRST["mlp"] + g * 64
                with dve.Fori(start, 8) as i:
                    mlp_tiles(g, i)
                if start == 1:
                    scale_of_rows(1)
                    dve.wait_ge(rstd_ready, 2)
                    nc.vector.tensor_tensor(rstd_sq[:, :], rstd[:, :], rstd[:, :],
                                            ALU.mult).then_inc(rstd_sq_ready, 1)
                    dve.wait_ge(rstd_sq_ready, 1)
                    dve.wait_ge(zeroed, 1)

                def add_group(n, b):
                    for t in range(NT):
                        if t == 0:
                            dve.wait_ge(half_group_done, g * 4 + (n + (GROUPS_BEFORE["mlp"] + 1)))
                        else:
                            dve.wait_ge(chunk_done, c + (n * 8 + 40))
                        dst = group_sum[:, t, bass.ds(n * GROUP_COLS, GROUP_COLS)]
                        nc.vector.scalar_tensor_tensor(out=dst, in0=group_bank[b][t][:, :],
                                                       scalar=rstd_sq[:, t:t + 1], in1=dst, op0=ALU.mult,
                                                       op1=ALU.add).then_inc(ff_sum_ready, 1)
                    dve.wait_ge(ff_sum_ready, g * 8 + (n * 2 + 2))
                    dve.sem_inc(group_taken[b], 1)

                if not last:
                    with dve.Fori(0, 2) as i:
                        for b in range(2):
                            rests(c + (i * 16 + (32 + 8 * b)), range(RING))
                            rests(c + (i * 16 + (36 + 8 * b)), range(RING))
                            add_group(i * 2 + b, b)
                    return
                for n in range(4):
                    cols_n = slice(n * GROUP_COLS, (n + 1) * GROUP_COLS)
                    rests(c + 32 + 8 * n, range(RING))
                    rests(c + 36 + 8 * n, range(RING - 1))
                    add_group(n, n % 2)
                    if n < 3:
                        rest(c + 39 + 8 * n, 3)
                    dve.wait_ge(rowg_in, 32)
                    for t in range(NT):
                        dve.wait_ge(ff_sq, 2 * n + t + 1)
                        if n == 3 and t == 1:
                            total_squares()
                        nc.vector.tensor_tensor(group_sum[:, t, cols_n], group_sum[:, t, cols_n],
                                                rowg[:, cols_n], ALU.mult).then_inc(group_gained, 1)

            mlp_tiles(0, 0)
            mlp_group(0, 1, False)
            with dve.Fori(1, FF_GROUPS - 1) as g:
                mlp_group(g, 0, False)
            mlp_group(FF_GROUPS - 1, 0, True)
            dve.wait_ge(group_gained, 16)
            dve.wait_ge(post_ready, 2)
            add_block(2, 0)
            add_block(2, 1)
            norm_block(2, 0)
            rest(FIRST["qkv"] - 1, 3)
            add_block(2, 2)
            norm_block(2, 1)
            add_block(2, 3)

            c = FIRST["qkv"]
            for n in range(2):
                for j in range(2 * n, 8):
                    if n == 0 and j + 2 < 8:
                        norm_block(2, j + 2)
                        if j < 4:
                            add_block(2, j + 4)
                    if n == 0 and j == 7:
                        scale_of_rows(2)
                    rest(c + 8 * n + j, j % RING)
                if n == 0:
                    diagonal(3)
                cols_n = slice(n * GROUP_COLS, (n + 1) * GROUP_COLS)
                for t in range(NT):
                    m = 2 * n + t
                    dve.wait_ge(vb_sq1, m + 1)
                    nc.vector.tensor_scalar(gelu_b[:, t, :], gelu_a[:, t, :], GELU_CUBE, 1.0, ALU.mult,
                                            ALU.add).then_inc(vb_step, 1)
                    dve.wait_ge(vb_step, m + 1)
                    nc.vector.tensor_tensor(gelu_b[:, t, :], gelu_b[:, t, :], vb[:, t, cols_n],
                                            ALU.mult).then_inc(vb_cube, 1)
                if n == 0:
                    rest(c + 8, 0)
                for t in range(NT):
                    m = 2 * n + t
                    dve.wait_ge(vb_tanh, m + 1)
                    nc.vector.scalar_tensor_tensor(out=vb[:, t, cols_n], in0=gelu_a[:, t, :], scalar=1.0,
                                                   in1=vb[:, t, cols_n], op0=ALU.add,
                                                   op1=ALU.mult).then_inc(vb_gelu, 1)
                if n == 0:
                    rest(c + 9, 1)
                for t in range(NT):
                    m = 2 * n + t
                    dve.wait_ge(vb_sq2, m + 1)
                    nc.vector.tensor_reduce(vb_sq[:, t, 4 * n:4 * n + 4],
                                            gelu_a[:, t, :].rearrange("p (h d) -> p h d", h=4), AX.X,
                                            ALU.add).then_inc(vb_sums, 1)
            keep_rows(2)
            dve.wait_ge(vb_sums, 4)
            dve.sem_inc(qkv_sums, 2)
            with dve.Fori(1, 4) as i:
                for g in range(2):
                    c_g = FIRST["qkv"] + (i * 16 + 8 * g)
                    rests(c_g, range(RING))
                    rests(c_g + 4, range(RING))
                    for t in range(NT):
                        m = i * 4 + (2 * g + t - 4)
                        dve.wait_ge(qkv_sq, m + 1)
                        nc.vector.tensor_scalar(qkv[:, t, bass.ds(i * 1024 + (g * 512 - 1024), GROUP_COLS)],
                                                group_bank[g][t][:, :], rstd[:, t:t + 1], None,
                                                ALU.mult).then_inc(qkv_in, 1)
                        nc.vector.tensor_reduce(head_sq[:, t, bass.ds(i * 8 + (4 * g - 8), 4)],
                                                gelu_a[:, t, :].rearrange("p (h d) -> p h d", h=4), AX.X,
                                                ALU.add).then_inc(qkv_sums, 1)
                    dve.wait_ge(qkv_in, i * 4 + (2 * g + 2 - 4))
                    dve.sem_inc(group_taken[g], 1)

            dve.wait_ge(rows_ready, 2)

            def scale_tile(b, c, g, summed=None):
                dve.wait_ge(chunk_done, c + 2)
                if summed is None:
                    nc.vector.tensor_tensor(uz_x[b], tile_sum[b][:, 0:TOK], rstd_rows[:, :],
                                            ALU.mult).then_inc(uz_scaled, 1)
                    dve.wait_ge(uz_scaled, g + 1)
                    dve.sem_inc(tile_taken[b], 1)
                    return
                add_halves(uz_x[b], tile_sum[b]).then_inc(uz_summed, 1)
                dve.wait_ge(uz_summed, summed + 1)
                dve.sem_inc(tile_taken[b], 1)
                nc.vector.tensor_tensor(uz_x[b], uz_x[b], rstd_rows[:, :], ALU.mult).then_inc(uz_scaled, 1)
                dve.wait_ge(uz_scaled, g + 1)

            with dve.Fori(0, 4) as i:
                for b in range(2):
                    g = i * 2 + b
                    c = FIRST["sgu_uz"] + (i * 4 + 2 * b)
                    rest(c, 2 * b)
                    scale_tile(b, c, g, g)
                    dve.wait_ge(uz_sq, g + 1)
                    nc.vector.tensor_scalar(uz_b[b], uz_a[b], GELU_CUBE, 1.0, ALU.mult, ALU.add).then_inc(uz_step, 1)
                    dve.wait_ge(uz_step, g + 1)
                    nc.vector.tensor_tensor(uz_a[b], uz_b[b], uz_x[b], ALU.mult).then_inc(uz_cube, 1)
                    rest(c + 1, 2 * b + 1)
                    dve.wait_ge(uz_tanh, g + 1)
                    nc.vector.scalar_tensor_tensor(out=one(u_gelu, g), in0=uz_b[b], scalar=1.0,
                                                   in1=uz_x[b], op0=ALU.add, op1=ALU.mult).then_inc(u_ready, 1)
            dve.wait_ge(scale_made, 2)
            dve.wait_ge(sgu_in, 32)
            with dve.Fori(0, 4) as i:
                for b in range(2):
                    g = i * 2 + b
                    c = FIRST["sgu_uz"] + 16 + (i * 4 + 2 * b)
                    dve.wait_ge(mix_done, g + 1)
                    for t in range(NT):
                        nc.vector.scalar_tensor_tensor(out=mixed[:, t * P:(t + 1) * P],
                                                       in0=mix_bank[b][:, t * P:(t + 1) * P], scalar=hscale[:, 2:3],
                                                       in1=one(b_s, g), op0=ALU.mult,
                                                       op1=ALU.add).then_inc(mixed_ready, 1)
                    rest(c, 2 * b)
                    scale_tile(b, c, g + 8)
                    dve.wait_ge(mixed_ready, g * 2 + 2)
                    nc.vector.scalar_tensor_tensor(out=mixed, in0=mixed, scalar=0.25, in1=one(u_gelu, g),
                                                   op0=ALU.mult, op1=ALU.mult).then_inc(mixed_u, 1)
                    dve.wait_ge(zb_tanh, g + 1)
                    nc.vector.scalar_tensor_tensor(out=uz_b[b], in0=uz_a[b], scalar=1.0, in1=uz_x[b],
                                                   op0=ALU.add, op1=ALU.mult).then_inc(zb_silu, 1)
                    dve.wait_ge(zb_silu, g + 1)
                    dve.wait_ge(mixed_u, g + 1)
                    nc.vector.tensor_tensor(uz_a[b], uz_b[b], mixed, ALU.mult).then_inc(sgu_f, 1)
                    rest(c + 1, 2 * b + 1)
                    dve.wait_ge(sgu_hi, g + 1)
                    nc.vector.tensor_tensor(one(a_lo, g + 8), uz_a[b], one(a_hi, g + 8).bitcast(F32),
                                            ALU.subtract).then_inc(sgu_ready, 1)
            with dve.Fori(0, 4) as i:
                for b in range(2):
                    g = i * 2 + b
                    c = FIRST["sgu_uz"] + 32 + (i * 4 + 2 * b)
                    rest(c, 2 * b)
                    scale_tile(b, c, g + 16, g + 8)
                    dve.wait_ge(za_tanh, g + 1)
                    nc.vector.scalar_tensor_tensor(out=one(za_silu, g), in0=uz_a[b], scalar=1.0,
                                                   in1=uz_x[b], op0=ALU.add, op1=ALU.mult).then_inc(za_ready, 1)
                    rest(c + 1, 2 * b + 1)

            def moba_gated(n):
                dve.wait_ge(pv_done, n + 1)
                nc.vector.scalar_tensor_tensor(out=att_f[:, :], in0=pv_sum[:, 0:TOK], scalar=0.5,
                                               in1=one(za_silu, n - FOX_HEADS), op0=ALU.mult,
                                               op1=ALU.mult).then_inc(att_f_ready, 1)

            def moba_att_lo(n):
                dve.wait_ge(att_hi, n + 1)
                dve.wait_ge(att_f_ready, n - 15)
                nc.vector.tensor_tensor(one(a_lo, n - FOX_HEADS), att_f[:, :],
                                        one(a_hi, n - FOX_HEADS).bitcast(F32),
                                        ALU.subtract).then_inc(att_ready, 1)

            def gate_head(h, first):
                n = h + FOX_HEADS

                def gate_tile(u, within=None):
                    c = FIRST["gates"] + h * 8 + 2 * u
                    slot = (2 * u) % RING
                    rest(c, slot)
                    if within is not None:
                        within(n)
                    dve.wait_ge(chunk_done, c + 2)
                    add_halves(one(gate, h * 4 + u), tile_sum[u % 2]).then_inc(gate_summed, 1)
                    dve.wait_ge(gate_summed, h * 4 + (u + 1))
                    dve.sem_inc(tile_taken[u % 2], 1)
                    nc.vector.tensor_tensor(one(gate, h * 4 + u), one(gate, h * 4 + u), rstd_rows[:, :],
                                            ALU.mult).then_inc(gate_scaled, 1)
                    rest(c + 1, slot + 1)

                gate_tile(0)
                dve.wait_ge(q_ready, n + 1)
                nc.vector.tensor_scalar(k_head[:, :], turned[:, TOK:2 * TOK], hcols[:, 1:2], None,
                                        ALU.mult).then_inc(k_ready, 1)
                if not first:
                    moba_gated(n - 1)
                gate_tile(1)
                soften(n, mask)
                if not first:
                    moba_att_lo(n - 1)
                gate_tile(2, normalise)
                gate_tile(3)

            dve.wait_ge(za_ready, 8)
            gate_head(0, True)
            with dve.Fori(1, MOBA_HEADS) as h:
                gate_head(h, False)

            dve.wait_ge(gate_ready, 32)
            def merge_tile(f, s):
                c = FIRST["proj_b"] + f
                dve.wait_ge(chunk_done, c + 1)
                add_halves(merge_t[s % 2], tile_sum[s % 2]).then_inc(mb_summed, 1)
                dve.wait_ge(mb_summed, f + 1)
                dve.sem_inc(tile_taken[s % 2], 1)
                nc.vector.scalar_tensor_tensor(out=one(merge_b, f), in0=one(gate, f + 16), scalar=1.0,
                                               in1=merge_t[s % 2], op0=ALU.add,
                                               op1=ALU.mult).then_inc(mb_ready, 1)
                rest(c, s)

            for s in range(4):
                merge_tile(s, s)
                if s == 1:
                    moba_gated(FOX_HEADS + MOBA_HEADS - 1)
                if s == 2:
                    moba_att_lo(FOX_HEADS + MOBA_HEADS - 1)
            with dve.Fori(1, 4) as i:
                for s in range(4):
                    merge_tile(i * 4 + s, s)
            with dve.Fori(0, 4) as i:
                for s in range(4):
                    f = i * 4 + s
                    c = FIRST["proj_a"] + f
                    dve.wait_ge(chunk_done, c + 1)
                    nc.vector.scalar_tensor_tensor(out=merge_t[s % 2], in0=one(gate, f), scalar=1.0,
                                                   in1=tile_sum[s % 2][:, 0:TOK], op0=ALU.add,
                                                   op1=ALU.mult).then_inc(ma_ready, 1)
                    dve.wait_ge(ma_ready, f + 1)
                    dve.wait_ge(mb_ready, 16)
                    dve.sem_inc(tile_taken[s % 2], 1)
                    nc.vector.tensor_tensor(merge_s[s % 2], merge_t[s % 2], one(merge_b, f),
                                            ALU.add).then_inc(merged_f, 1)
                    rest(c, s)
                    dve.wait_ge(merged_hi, f + 1)
                    nc.vector.scalar_tensor_tensor(out=one(h_lo, f), in0=merge_s[s % 2], scalar=0.5,
                                                   in1=one(h_hi, f).bitcast(F32), op0=ALU.mult,
                                                   op1=ALU.subtract).then_inc(merged_ready, 1)
            c = FIRST["out"]
            for n in range(4):
                cols_n = slice(n * GROUP_COLS, (n + 1) * GROUP_COLS)
                for j in range(8):
                    if 8 * n + j < 32 - RING:
                        rest(c + 8 * n + j, j % RING)
                for t in range(NT):
                    if t == 0:
                        dve.wait_ge(half_group_done, GROUPS_BEFORE["out"] + n + 1)
                    else:
                        dve.wait_ge(chunk_done, c + 8 * n + 8)
                    nc.vector.tensor_tensor(group_sum[:, t, cols_n], group_bank[n % 2][t][:, :],
                                            res[:, t, cols_n], ALU.add).then_inc(out_ready, 1)
                dve.wait_ge(out_ready, 2 * n + 2)
                dve.sem_inc(group_taken[n % 2], 1)

        @block.gpsimd
        def _(pool):
            nc.gpsimd.memset(half_neg[:, :], -0.5).then_inc(consts_made, 1)
            nc.gpsimd.memset(ident[:, :], 0.0).then_inc(consts_made, 1)
            pool.wait_ge(consts_made, 2)
            nc.gpsimd.affine_select(out=ident[:, :], in_=ident[:, :], compare_op=ALU.not_equal, fill=1.0, base=0,
                                    pattern=[[-1, P]], channel_multiplier=1).then_inc(consts_made, 1)
            nc.gpsimd.memset(ones[:, :], 1.0).then_inc(consts_made, 1)
            for part in f_zero:
                nc.gpsimd.memset(part.bitcast(F32), 0.0).then_inc(f_zeroed, 1)

            def pow_norm(dst, n, var, ready):
                nc.gpsimd.tensor_scalar(mean_sq[:, :], sq_all[:, :], 1.0 / D, EPS, ALU.mult,
                                        ALU.add).then_inc(var, 1)
                pool.wait_ge(var, n)
                nc.gpsimd.tensor_tensor(dst[:, :], mean_sq[:, :], half_neg[:, 0:2], ALU.pow).then_inc(ready, 1)

            pool.wait_ge(consts_made, 4)

            nc.gpsimd.memset(mask[:, :], 0.0).then_inc(consts_made, 1)
            pool.wait_ge(consts_made, 5)
            for b in (0, 2):
                blk = mask[:, b * P:(b + 1) * P]
                nc.gpsimd.affine_select(out=blk, in_=blk, compare_op=ALU.is_ge, fill=NEG, base=0,
                                        pattern=[[-1, P]], channel_multiplier=1).then_inc(consts_made, 1)
            nc.gpsimd.memset(tri, 1.0).then_inc(consts_made, 1)
            pool.wait_ge(consts_made, 8)
            nc.gpsimd.affine_select(out=tri, in_=tri, compare_op=ALU.is_ge, fill=0.0, base=0,
                                    pattern=[[-P, NT], [1, TOK]], channel_multiplier=-1).then_inc(tri_made, 1)
            pool.wait_ge(hcols_in, 16)
            nc.gpsimd.tensor_scalar(hscale[:, 0:1], hcols[:, 0:1], SCALE, 1.0, ALU.mult,
                                    ALU.mult).then_inc(scale_made, 1)
            nc.gpsimd.tensor_scalar(hscale[:, 2:3], hcols[:, 2:3], 0.5, 1.0, ALU.mult,
                                    ALU.mult).then_inc(scale_made, 1)
            pool.wait_ge(mean_ready, 1)
            pow_norm(rstd, 1, var_ready, rstd_ready)
            pool.dma_start(rowg[:, :], norm_rows[0:1, :].broadcast_to([P, D])).then_inc(rowg_in, 16)

            pool.wait_ge(cum_ready, 2)
            pool.dma_start(fox_scratch, cum_neg).then_inc(cum_out, 16)
            pool.wait_ge(cum_out, 16)
            pool.dma_start(cum_rows.rearrange("p h t -> p (h t)"),
                           fox_scratch.rearrange("(o h) t -> o (h t)", o=1).broadcast_to([P, FOX_HEADS * TOK])
                           ).then_inc(cum_in, 16)
            pool.wait_ge(cum_in, 16)
            pool.wait_ge(v_ready, 8)

            def stage_fox(h, first):
                if not first:
                    pool.wait_ge(logit_ready, h)
                c0, c1 = [one(cum_cols[:, t:t + 1, :].rearrange("p a h -> p h a"), h) for t in range(NT)]
                rows = one(cum_rows, h)
                nc.gpsimd.tensor_tensor(bias[:, 0:P], rows[:, 0:P], c0.broadcast_to([P, P]),
                                        ALU.add).then_inc(bias_step, 1)
                nc.gpsimd.tensor_tensor(bias[:, P:384], rows, c1.broadcast_to([P, TOK]),
                                        ALU.add).then_inc(bias_step, 1)
                pool.wait_ge(bias_step, h * 2 + 2)
                nc.gpsimd.tensor_tensor(bias[:, :], bias[:, :], mask[:, :], ALU.add).then_inc(bias_ready, 1)
                if not first:
                    pool.wait_ge(pv_done, h)
                nc.gpsimd.tensor_copy(v_head[:, :, :], fox_v[:, :, bass.ds(h * P, P)]).then_inc(v_head_ready, 1)

            stage_fox(0, True)
            with pool.Fori(1, FOX_HEADS) as h:
                stage_fox(h, False)

            pool.wait_ge(post_mean, 1)
            pow_norm(post_rstd, 1, post_var, post_ready)
            pool.wait_ge(res_added, 16)
            nc.gpsimd.memset(wide[:, 0:NT * D], 0.0).then_inc(zeroed, 1)
            pool.wait_ge(mean_ready, 2)
            pow_norm(rstd, 2, var_ready, rstd_ready)
            pool.dma_start(rowg[:, :], norm_rows[1:2, :].broadcast_to([P, D])).then_inc(rowg_in, 16)

            pool.wait_ge(post_mean, 2)
            pow_norm(post_rstd, 2, post_var, post_ready)
            pool.dma_start(w_s, w_spatial).then_inc(sgu_in, 16)
            pool.dma_start(b_s.rearrange("p g t -> p (g t)"), b_spatial.broadcast_to([P, 1024])).then_inc(sgu_in, 16)
            pool.wait_ge(mean_ready, 3)
            pow_norm(rstd, 3, var_ready, rstd_ready)
            pool.wait_ge(sgu_in, 32)
            nc.gpsimd.affine_select(out=w_s, in_=w_s, compare_op=ALU.is_ge, fill=0.0, base=0,
                                    pattern=[[0, 8], [1, P]], channel_multiplier=-1).then_inc(w_s_ready, 1)

            pool.wait_ge(vb_sums, 4)
            nc.gpsimd.tensor_scalar(vb_sq[:, :, :], vb_sq[:, :, :], 0.25 / P, EPS, ALU.mult,
                                    ALU.add).then_inc(hvar, 1)
            pool.wait_ge(hvar, 1)
            nc.gpsimd.tensor_tensor(vb_rstd[:, :, :].rearrange("p t h -> p (t h)"),
                                    vb_sq[:, :, :].rearrange("p t h -> p (t h)"), half_neg[:, 0:16],
                                    ALU.pow).then_inc(hr_ready, 1)
            pool.wait_ge(hr_ready, 1)

            def rows_by_head(dst, src, r, h):
                for t in range(NT):
                    s = src[:, t, bass.ds(h * P, P)]
                    c = r[:, t, bass.ds(h, 1)].broadcast_to([P, P])
                    ins = nc.gpsimd.tensor_tensor(dst[:, t, :], s, c, ALU.mult)
                return ins

            pool.wait_ge(pv_done, FOX_HEADS)
            for b in range(2):
                rows_by_head(vb_head[b], vb, vb_rstd, b).then_inc(vb_head_ready, 1)
            with pool.Fori(1, 4) as i:
                for b in range(2):
                    pool.wait_ge(mixed_ready, i * 4 + (2 * b - 2))
                    rows_by_head(vb_head[b], vb, vb_rstd, i * 2 + b).then_inc(vb_head_ready, 1)

            pool.wait_ge(qkv_sums, 14)
            nc.gpsimd.tensor_scalar(head_sq[:, :, :], head_sq[:, :, :], 1.0 / P, EPS, ALU.mult,
                                    ALU.add).then_inc(hvar, 1)
            pool.wait_ge(hvar, 2)
            nc.gpsimd.tensor_tensor(head_rstd[:, :, :].rearrange("p t h -> p (t h)"),
                                    head_sq[:, :, :].rearrange("p t h -> p (t h)"), half_neg[:, :],
                                    ALU.pow).then_inc(hr_ready, 1)
            pool.wait_ge(hr_ready, 2)

            def stage_moba(h, first):
                if not first:
                    pool.wait_ge(qk_turned, h)
                rows_by_head(qk_norm[:, 0:2, :], qkv, head_rstd, h).then_inc(qk_norm_ready, 1)
                rows_by_head(qk_norm[:, 2:4, :], qkv, head_rstd, h + 8).then_inc(qk_norm_ready, 1)
                if first:
                    pool.wait_ge(mixed_ready, 16)
                else:
                    pool.wait_ge(pv_done, h + FOX_HEADS)
                nc.gpsimd.tensor_copy(v_head[:, :, :],
                                      qkv[:, :, bass.ds(h * P + 2048, P)]).then_inc(v_head_ready, 1)

            stage_moba(0, True)
            with pool.Fori(1, MOBA_HEADS) as h:
                stage_moba(h, False)


def feature_tiles(w):
    k, f = w.shape
    return w.reshape(k // 1024, 8, P, f // P, P).transpose(3, 0, 2, 1, 4).reshape(-1, P, CHUNK)


def token_groups(w):
    k, f = w.shape
    return w.reshape(k // 256, 2, P, f // GROUP_COLS, GROUP_COLS).transpose(3, 0, 2, 1, 4).reshape(-1, P, CHUNK)


def kernel(**inputs):
    import numpy as np
    import concourse.bacc as bacc
    from concourse.bass_utils import run_bass_kernel_spmd

    a = {k: np.asarray(v) for k, v in inputs.items()}
    fox = a["fox_w_in"][0]
    w1, w2, w2nd = a["mlp_w1"][0], a["mlp_w2"][0], a["w_in_2"][0]
    q, k, v, z_a, u_b, v_b, z_b = [w2nd[:, n * 1024:(n + 1) * 1024] for n in range(7)]
    fox_q = feature_tiles(fox[:, 0:D]).reshape(FOX_HEADS, TILE_CHUNKS, P, CHUNK)
    fox_k = feature_tiles(fox[:, D:2 * D]).reshape(FOX_HEADS, TILE_CHUNKS, P, CHUNK)
    parts = [
        token_groups(fox[:, 2 * D:3 * D]),
        np.stack([fox_q, fox_k], axis=1).reshape(-1, P, CHUNK),
        token_groups(a["fox_w_out"][0]),
    ]
    for g in range(FF_GROUPS):
        parts += [feature_tiles(w1[:, g * D:(g + 1) * D]), token_groups(w2[g * D:(g + 1) * D, :])]
    parts += [token_groups(m) for m in (v_b, q, k, v)]
    parts += [feature_tiles(m) for m in (u_b, z_b, z_a, w2nd[:, 7168:], a["w_proj_b_2"][0], a["w_proj_a_2"][0])]
    parts += [token_groups(a["w_out_2"][0])]
    by_feature = lambda g: g.reshape(KT, P).T
    arrays = {
        "stream": np.concatenate(parts, axis=0),
        "x": a["x"],
        "fox_w_f": np.ascontiguousarray(fox[:, 3 * D:].reshape(KT, P, FOX_HEADS).transpose(1, 0, 2)),
        "fox_b_f": a["fox_b_f"],
        "norm_rows": np.ascontiguousarray(a["norm_g"][0][[1, 3]]),
        "norm_cols": np.ascontiguousarray(np.stack(
            [by_feature(a["norm_g"][0, 0]), by_feature(a["norm_g"][0, 2]), by_feature(a["norm_g_2"][0])], axis=1)),
        "w_spatial": np.ascontiguousarray(a["w_spatial_2"][0].transpose(2, 0, 1)),
        "b_spatial": np.ascontiguousarray(a["b_spatial_2"][0].reshape(1, 1024)),
        "head_cols": np.ascontiguousarray(np.stack(
            [a["q_norm_g_2"][0], a["k_norm_g_2"][0], a["sgu_norm_g_2"][0]], axis=1)),
    }
    nc = bacc.Bacc("TRN2", target_bir_lowering=False, num_devices=1)
    aps = [nc.dram_tensor(f"in_{name}", v.shape, mybir.dt.from_np(v.dtype), kind="ExternalInput").ap()
           for name, v in arrays.items()]
    out = nc.dram_tensor("out", (1, TOK, D), F32, kind="ExternalOutput").ap()
    build(nc, *aps, out)
    r = run_bass_kernel_spmd(nc, [{f"in_{name}": v for name, v in arrays.items()}], core_ids=[0])
    return r.results[0]["out"]
```
